# Optimizing a Trainium2 kernel written in Bass

```python
import jax, jax.numpy as jnp
from jax import lax
import numpy as np

D_MODEL = 1024
BATCH = 1
SEQ = 256
DEPTH = 2

CHUNK = 64
Q_BLOCK = 128
EPS = 1e-6

A_HEADS = 8
A_HEAD_DIM = 64
A_WIDTH = A_HEADS * A_HEAD_DIM
KV_LATENT = 128
IDX_HEADS = 8
IDX_DIM = 64
TOPK_MAX = 256

B_WIDTH = D_MODEL - A_WIDTH
B_GROUPS = 4
B_GROUP_DIM = B_WIDTH // B_GROUPS
SGU_CHUNK = 128

POOL_WINDOWS = (2, 4, 8, 16)
C_GROUPS = len(POOL_WINDOWS)
C_GROUP_DIM = D_MODEL // C_GROUPS

N_GROUPS = 4
EXPERTS_PER_GROUP = 8
N_EXPERTS = N_GROUPS * EXPERTS_PER_GROUP
TOP_K_IN_GROUP = 2
D_EXPERT = 256

IN_SIZES = (A_WIDTH, KV_LATENT, IDX_HEADS * IDX_DIM, IDX_DIM, IDX_HEADS, B_WIDTH, B_WIDTH)
D_IN = sum(IN_SIZES)
IN_OFFSETS = tuple(int(o) for o in np.cumsum(IN_SIZES)[:-1])

N_EVEN = (DEPTH + 1) // 2
N_ODD = DEPTH // 2

kernel_name = "hybrid_dsa_sgu_pool_hmoe_trunk"

def rmsnorm(x, g):
    xf = x.astype(jnp.float32)
    y = xf * lax.rsqrt(jnp.mean(xf * xf, axis=-1, keepdims=True) + EPS)
    return (y * g.astype(jnp.float32)).astype(x.dtype)

def layernorm(x, g):
    xf = x.astype(jnp.float32)
    mu = jnp.mean(xf, axis=-1, keepdims=True)
    var = jnp.mean(jnp.square(xf - mu), axis=-1, keepdims=True)
    return ((xf - mu) * lax.rsqrt(var + EPS) * g.astype(jnp.float32)).astype(x.dtype)

def modulate(h, shift, scale):
    return h * (1 + scale[:, None, :]) + shift[:, None, :]

def alibi_slopes(n):
    return jnp.asarray(np.array([2.0 ** (-8.0 * (i + 1) / n) for i in range(n)], dtype=np.float32))

def dsa_attention(q, k, v, q_idx, k_idx, w_idx):
    B, S = q.shape[0], q.shape[1]
    topk = min(TOPK_MAX, S // 4)
    nb = S // Q_BLOCK
    slopes = alibi_slopes(A_HEADS)
    key_pos = jnp.arange(S)
    kv = jnp.concatenate([k, v], axis=-1)

    def to_blocks(a):
        return jnp.moveaxis(a.reshape((B, nb, Q_BLOCK) + a.shape[2:]), 1, 0)

    def block(args):
        qb, qib, wib, qpos = args
        logits = jnp.einsum('bqhd,bsd->bqhs', qib, k_idx) * (IDX_DIM ** -0.5)
        score = jnp.einsum('bqhs,bqh->bqs', jax.nn.relu(logits), wib).astype(jnp.float32)
        visible = (key_pos[None, :] // CHUNK) <= (qpos[:, None] // CHUNK)
        score = jnp.where(visible[None], score, -jnp.inf)
        _, idx = lax.top_k(score, topk)
        valid = (idx // CHUNK) <= (qpos[None, :, None] // CHUNK)
        kv_sel = jax.vmap(lambda kk, ii: kk[ii])(kv, idx)
        k_sel, v_sel = jnp.split(kv_sel, 2, axis=-1)
        att = jnp.einsum('bqhd,bqkd->bqhk', qb, k_sel).astype(jnp.float32) * (A_HEAD_DIM ** -0.5)
        dist = jnp.abs(qpos[None, :, None] - idx).astype(jnp.float32)
        att = att - slopes[None, None, :, None] * dist[:, :, None, :]
        att = jnp.where(valid[:, :, None, :], att, -jnp.inf)
        p = jax.nn.softmax(att, axis=-1).astype(v.dtype)
        return jnp.einsum('bqhk,bqkd->bqhd', p, v_sel)

    out = lax.map(block, (to_blocks(q), to_blocks(q_idx), to_blocks(w_idx),
                          jnp.arange(S).reshape(nb, Q_BLOCK)))
    return jnp.moveaxis(out, 0, 1).reshape(B, S, A_WIDTH)

def spatial_gating(u, v, ln_g, w_s, b_s):
    B, S, _ = u.shape
    u = jax.nn.gelu(u)
    v = layernorm(jax.nn.gelu(v), ln_g)
    nc = S // SGU_CHUNK
    vg = v.reshape(B, nc, SGU_CHUNK, B_GROUPS, B_GROUP_DIM)
    pos = jnp.arange(SGU_CHUNK)
    mask = (pos[None, :] // CHUNK) <= (pos[:, None] // CHUNK)
    w = jnp.where(mask[None], w_s, jnp.zeros_like(w_s))
    mixed = jnp.einsum('gij,bnjgc->bnigc', w, vg) + b_s.T[None, None, :, :, None]
    return u * mixed.reshape(B, S, B_WIDTH)

def hybrid_ab(h, w_in, kv_norm, w_kv_up, sgu_norm, w_s, b_s, w_o):
    B, S, _ = h.shape
    proj = h @ w_in
    q, kv_lat, q_idx, k_idx, w_idx, u, v = jnp.split(proj, IN_OFFSETS, axis=-1)
    kv = rmsnorm(kv_lat, kv_norm) @ w_kv_up
    k, v_att = jnp.split(kv, 2, axis=-1)
    a_out = dsa_attention(q.reshape(B, S, A_HEADS, A_HEAD_DIM), k, v_att,
                          q_idx.reshape(B, S, IDX_HEADS, IDX_DIM), k_idx,
                          w_idx * (IDX_HEADS ** -0.5))
    b_out = spatial_gating(u, v, sgu_norm, w_s, b_s)
    return jnp.concatenate([a_out, b_out], axis=-1) @ w_o

def multiscale_pool(h, w_pool, scale):
    B, S, D = h.shape
    hf = h.astype(jnp.float32).reshape(B, S, C_GROUPS, C_GROUP_DIM)
    cs = jnp.concatenate([jnp.zeros((B, 1, C_GROUPS, C_GROUP_DIM), jnp.float32),
                          jnp.cumsum(hf, axis=1)], axis=1)
    t = jnp.arange(S)
    pooled = []
    for g, win in enumerate(POOL_WINDOWS):
        start = jnp.maximum(t + 1 - win, 0)
        cnt = (t + 1 - start).astype(jnp.float32)
        pooled.append((cs[:, 1:, g] - cs[:, start, g]) / cnt[None, :, None])
    y = (jnp.stack(pooled, axis=2) - hf).astype(h.dtype)
    y = jnp.einsum('bsgc,gce->bsge', y, w_pool).reshape(B, S, D)
    return y * scale

def hier_moe(h, w_gr, b_gr, w_er, b_er, w_gate, w_up, w_down):
    def per_seq(t):
        S = t.shape[0]
        g_logits = (t @ w_gr).astype(jnp.float32) + b_gr.astype(jnp.float32)
        g_prob = jax.nn.softmax(g_logits, axis=-1)
        g_sel = jnp.argmax(g_logits, axis=-1)
        p_g = jnp.take_along_axis(g_prob, g_sel[:, None], axis=1)
        e_logits = ((t @ w_er).astype(jnp.float32) + b_er.astype(jnp.float32)).reshape(S, N_GROUPS, EXPERTS_PER_GROUP)
        e_in_group = jnp.take_along_axis(e_logits, g_sel[:, None, None], axis=1)[:, 0]
        top_val, top_idx = lax.top_k(e_in_group, TOP_K_IN_GROUP)
        gate = p_g * jax.nn.softmax(top_val, axis=-1)
        expert_id = g_sel[:, None] * EXPERTS_PER_GROUP + top_idx
        combine = jnp.sum(jax.nn.one_hot(expert_id, N_EXPERTS, dtype=jnp.float32) * gate[..., None], axis=1)
        hg = jnp.einsum('sd,edf->sef', t, w_gate)
        hu = jnp.einsum('sd,edf->sef', t, w_up)
        act = jax.nn.silu(hg) * hu * combine[:, :, None].astype(t.dtype)
        return jnp.einsum('sef,efd->sd', act, w_down)
    return lax.map(per_seq, h)

def setup_inputs(seed: int = 0) -> dict:
    key = jax.random.key(seed)
    ks = iter(jax.random.split(key, 32))
    f32 = jnp.float32
    D = D_MODEL

    def nrm(shape, scale):
        return jax.random.normal(next(ks), shape, f32) * scale

    def gain(shape):
        return 1.0 + 0.02 * jax.random.normal(next(ks), shape, f32)

    return {
        "x": nrm((BATCH, SEQ, D), 1.0),
        "c": nrm((BATCH, D), 1.0),
        "w_mod": nrm((DEPTH, D, 6 * D), 0.5 * D ** -0.5),
        "b_mod": nrm((DEPTH, 6 * D), 0.02),
        "norm_mix": gain((DEPTH, D)),
        "norm_ffn": gain((DEPTH, D)),
        "w_in": nrm((N_EVEN, D, D_IN), D ** -0.5),
        "kv_norm": gain((N_EVEN, KV_LATENT)),
        "w_kv_up": nrm((N_EVEN, KV_LATENT, 2 * A_HEAD_DIM), KV_LATENT ** -0.5),
        "sgu_norm": gain((N_EVEN, B_WIDTH)),
        "w_s": nrm((N_EVEN, B_GROUPS, SGU_CHUNK, SGU_CHUNK), SGU_CHUNK ** -0.5),
        "b_s": gain((N_EVEN, B_GROUPS, SGU_CHUNK)),
        "w_o": nrm((N_EVEN, D, D), D ** -0.5),
        "w_pool": nrm((N_ODD, C_GROUPS, C_GROUP_DIM, C_GROUP_DIM), C_GROUP_DIM ** -0.5),
        "pool_scale": gain((N_ODD, D)),
        "w_gr": nrm((DEPTH, D, N_GROUPS), D ** -0.5),
        "b_gr": nrm((DEPTH, N_GROUPS), 0.01),
        "w_er": nrm((DEPTH, D, N_EXPERTS), D ** -0.5),
        "b_er": nrm((DEPTH, N_EXPERTS), 0.01),
        "w_gate": nrm((DEPTH, N_EXPERTS, D, D_EXPERT), D ** -0.5),
        "w_up": nrm((DEPTH, N_EXPERTS, D, D_EXPERT), D ** -0.5),
        "w_down": nrm((DEPTH, N_EXPERTS, D_EXPERT, D), D_EXPERT ** -0.5),
        "norm_out": gain((D,)),
    }

def reference(x, c, w_mod, b_mod, norm_mix, norm_ffn, w_in, kv_norm, w_kv_up, sgu_norm,
              w_s, b_s, w_o, w_pool, pool_scale, w_gr, b_gr, w_er, b_er,
              w_gate, w_up, w_down, norm_out):
    cs = jax.nn.silu(c)
    for i in range(DEPTH):
        mod = cs @ w_mod[i] + b_mod[i]
        sh_m, sc_m, g_m, sh_f, sc_f, g_f = jnp.split(mod, 6, axis=-1)
        h = modulate(rmsnorm(x, norm_mix[i]), sh_m, sc_m)
        j = i // 2
        if i % 2 == 0:
            y = hybrid_ab(h, w_in[j], kv_norm[j], w_kv_up[j], sgu_norm[j], w_s[j], b_s[j], w_o[j])
        else:
            y = multiscale_pool(h, w_pool[j], pool_scale[j])
        x = x + g_m[:, None, :] * y
        h = modulate(rmsnorm(x, norm_ffn[i]), sh_f, sc_f)
        x = x + g_f[:, None, :] * hier_moe(h, w_gr[i], b_gr[i], w_er[i], b_er[i],
                                           w_gate[i], w_up[i], w_down[i])
    return rmsnorm(x, norm_out)


_drawn_inputs = setup_inputs


def setup_inputs(seed=0):
    import zlib

    import numpy as np

    out = dict(_drawn_inputs(seed))
    spreads = {}
    factors = {'norm_mix': 3.066,
     'norm_ffn': 4.151,
     'kv_norm': 8.0,
     'sgu_norm': 8.0,
     'b_s': 7.337,
     'pool_scale': 5.902,
     'b_gr': 5.43,
     'b_er': 6.461,
     'norm_out': 2.812}
    for name, (base, spread) in spreads.items():
        noise = np.random.default_rng([zlib.crc32(name.encode()), seed]).standard_normal(out[name].shape)
        drawn = base * np.exp(spread * noise) if base else spread * noise
        out[name] = __import__('jax').numpy.asarray(drawn.astype(out[name].dtype))
    for name, factor in factors.items():
        out[name] = (out[name] * factor).astype(out[name].dtype)
    return out
```

```python
from contextlib import ExitStack

import concourse.bass as bass
from concourse import mybir

F32 = mybir.dt.float32
I32 = mybir.dt.int32
ALU = mybir.AluOpType
ACT = mybir.ActivationFunctionType
AX = mybir.AxisListType.X

P = 128
EPS = 1e-6
CHUNK = 64
GELU_A, GELU_C = 0.044715, 0.7978845608028654
NEVER = -(2.0 ** 126)
TAKEN = -(2.0 ** 127)
FAR = -(2.0 ** 100)


def trunk(nc, x, c, w_mod, b_mod, norm_mix, norm_ffn, w_in, kv_norm, w_kv_up, sgu_norm, w_s, b_s, w_o,
          w_pool, pool_scale, w_gr, b_gr, w_er, b_er, w_gate, w_up, w_down, norm_out, out):
    T, D = x.shape[1:]
    L, NE, _, FE = w_gate.shape
    NG = w_gr.shape[2]
    EG = NE // NG
    TT, KT, FT = T // P, D // P, FE // P
    H, HD = 8, 64
    LAT = kv_norm.shape[1]
    HALF = 512
    SLOTS = 2 * T
    WIN = P
    PADDED = SLOTS + WIN
    TOPK = min(256, T // 4)
    BW = w_s.shape[1] * P
    Q0, KV0, QI0, KI0, U0, V0 = 0, 512, 640, 1152, 1224, 1736
    RCOLS = NG + NE
    assert (T, D, L, NE, FE, NG, LAT, BW) == (256, 1024, 2, 32, 256, 4, 128, 512)

    with ExitStack() as ctx:
        def sb(name, shape, dt=F32):
            return ctx.enter_context(nc.sbuf_tensor(name, shape, dt))

        def sem(name):
            return ctx.enter_context(nc.semaphore(name))

        CH = 6
        XS = 4
        ring = sb("ring", [P, CH * KT * HALF])
        x_res = sb("x_res", [P, TT, D])
        xn = sb("xn", [P, TT, D])
        hT = sb("hT", [P, KT, T])
        gates = sb("gates", [P, 4, D])
        arena = sb("arena", [P, 11520])
        wpool = sb("wpool", [P, 4, 2, 256])
        ident = sb("ident", [P, P])
        ones = sb("ones", [P, P])
        before = sb("before", [P, P])
        slot_no = sb("slot_no", [P, SLOTS])
        rows = sb("rows", [9, D])
        row_sel = sb("row_sel", [9, 6, P])
        wroute = sb("wroute", [P, L, KT, RCOLS])
        broute = sb("broute", [P, L, RCOLS])
        bias_col = sb("bias_col", [P, L, 6, KT])
        gain_col = sb("gain_col", [P, 4, KT])
        kvg = sb("kvg", [P, 1])
        sgug = sb("sgug", [P, 4])
        raw_col = sb("raw_col", [P, 8, KT])
        ab = sb("ab", [P, L, 4, KT])
        cs = sb("cs", [P, 3, KT])
        stat = sb("stat", [P, 32])
        mhalf = sb("mhalf", [P, 2])
        w8 = sb("w8", [P, TT, H])
        best = sb("best", [P, 8])
        amax = sb("amax", [P, TT, H])
        asum = sb("asum", [P, TT, H])
        edge = sb("edge", [P, 16])
        rank = sb("rank", [P, 8])
        rt = sb("rt", [P, 728])
        win_i = sb("win_i", [1, 2 * NE], I32)
        eid_i = sb("eid_i", [1, 2 * NE], I32)
        grp_i = sb("grp_i", [1, L], I32)

        def chunk_at(n):
            s = (n % CH) * KT * HALF
            return ring[:, s:s + KT * HALF].rearrange("p (k n) -> p k n", k=KT)

        EW = 3 * KT * FE

        def gu_at(s):
            return ring[:, s * EW:s * EW + 2 * KT * FE].rearrange("p (w k f) -> p w k f", w=2, k=KT)

        def dn_at(s):
            return ring[:, s * EW + 2 * KT * FE:(s + 1) * EW].rearrange("p (t d) -> p t d", t=FT)

        def ar(a, n, **kw):
            v = arena[:, a:a + n]
            if kw:
                names = " ".join(kw)
                v = v.rearrange(f"p ({names} z) -> p {names} z", **kw)
            return v

        qiT, gtmp, qT, uT = ar(0, 1024, t=4), ar(1024, 1024, t=2), ar(2048, 1024, t=4), ar(3072, 1024, t=4)
        pT0, pT1 = ar(0, 1024), ar(0, 2048, s=2)
        vtk = ar(4096, 1024, t=2)
        att0 = ar(5120, 1024, h=8)
        kvn, kvnT, kidup = ar(5120, 256, t=2), ar(5376, 256), ar(5632, 256, t=2)
        relu = ar(6144, 1024, b=2)
        wkv = ar(3584, 384, w=3)
        ws_raw, usq = ar(3072, 512, g=4), ar(0, 1024, t=4)
        csb = ar(7168, 1024, k=8)
        score, keep, dist = ar(8192, 512, t=2), ar(8704, 512, t=2), ar(9216, 512, t=2)
        bsb, wsT = ar(9728, 512, g=4), ar(10240, 512, g=4)
        kiT, kT, v2 = ar(10752, 256), ar(11008, 256), ar(11264, 256, t=2)
        att1 = hT[:, :, :].rearrange("p k t -> p (k t)").rearrange("p (h s) -> p h s", h=8)
        xnf = xn[:, :, :].rearrange("p a b -> p (a b)")
        catT = xnf.rearrange("p (k t) -> p k t", k=8)
        xgT, yT, combT = ar(0, KT * PADDED, k=8), ar(5120, KT * PADDED, k=8), ar(10240, 1024, s=4)
        sel, comb, pick = ar(5120, 1024, t=2), ar(6144, 1024, t=2), ar(8192, 1024, t=2)
        ysl = ar(0, 4096, s=4)
        xw = xnf.rearrange("p (b k s) -> p b k s", b=2, k=KT)
        hflat = hT[:, :, :].rearrange("p k t -> p (k t)")
        th = hflat[:, 0:512].rearrange("p (b f) -> p b f", b=2)
        gl = hflat[:, 512:1024].rearrange("p (b f) -> p b f", b=2)
        act_s = hflat[:, 1024:1536].rearrange("p (b t f) -> p b t f", b=2, t=FT)
        actT = hflat[:, 1536:2048].rearrange("p (b t s) -> p b t s", b=2, t=FT)
        PAD = 16
        hp, sA, sB = ar(0, 2176, k=8), ar(2176, 2176, k=8), ar(4352, 2176, k=8)

        def v3(a, n):
            return rt[:, a:a + TT * n].rearrange("p (t n) -> p t n", t=TT)

        rt_gd, rt_ge, rt_dd, rt_q, rt_m = rt[:, 74:82], rt[:, 82:90], rt[:, 260:262], rt[:, 262:264], rt[:, 110:112]
        asg1, asg2, asg, tot = v3(270, NE), v3(334, NE), v3(398, NE), rt[:, 526:526 + P]

        bank = [ctx.enter_context(nc.psum_tensor(f"bank{i}", [P, 512], F32)) for i in range(8)]

        mods = [(l, v) for l in range(L) for v in range(6)]
        plan = [("mod", m) for m in range(4)] + [("in", "qi"), ("in", "kv"), ("in", "q"), ("in", "v"), ("in", "u")]
        plan += [("mod", 4), ("mod", 5), ("out", 0), ("out", 1)] + [("mod", m) for m in range(6, 24)]
        chunk_no = {key: n for n, key in enumerate(plan)}
        chunk_dmas = [2 if key == ("in", "kv") else 1 for key in plan]

        def arrivals(n):
            return 16 * sum(chunk_dmas[i] for i in range(n % CH, n + 1, CH))

        GATE = {(0, 2): 0, (0, 5): 1, (1, 2): 2, (1, 5): 3}
        columns = [v for v in mods if v not in GATE]
        ROW_BIAS = {(0, 2): 0, (0, 5): 1, (1, 2): 2, (1, 5): 3, (1, 0): 7, (1, 1): 8}

        names = """c_in x_in early_in small_in late_in consts c_tanh csb_ready
            chunk_done mod_kept col_done col_kept ab_ready
            square_sum mean_sq inv_rms xn_ready xT_done hT_act hT_dve x_ready
            ws_turned wsT_copied wsT_ready gain_row gain_ready
            qi_done qi_kept kv_sq kv_ms kv_inv wkv_ready kv_ready kt_turned kiT_ready kvnT_ready
            kup_done kup_kept q_done q_kept v_done v_kept v_poly v_tanh ln_ms ln_inv vln_ready
            u_done u_kept u_poly u_tanh u_ready score_done score_relu score_added
            att_done att_shift att_exp att_ready p_turned pT_ready pv_done cat_act cat_dve
            mix_done sgu_done bT_ready
            lg_done g_shift e_group e_pair_in e_pair asg_ready tot_done tot_ready off_done
            sel_ready comb_ready xg_done xg_act xg_dve win_ready comb_turned combT_ready
            row_done row_kept pool_ready y_turned ysl_act ysl_dve out_ready out_stored dve_own pool_own""".split()
        S = {n: sem(n) for n in names}
        chunk_in = [sem(f"chunk_in{i}") for i in range(CH)]
        gu_in = [[sem(f"gu_in{l}_{i}") for i in range(XS)] for l in range(L)]
        dn_in = [[sem(f"dn_in{l}_{i}") for i in range(XS)] for l in range(L)]
        E = [{n: sem(f"{n}{l}") for n in ("xw_ready", "gu_done", "gu_tanh", "gl_ready", "act_ready", "act_turned", "actT_ready",
                                          "down_done", "y_act", "y_dve", "y_last_act", "y_last_dve")} for l in range(L)]

        def head_at(place):
            return 2 * (place % (H // 2)) + place // (H // 2)

        def xslot(j):
            return (j + 1) % XS

        EARLY, SMALL, LATE = 4, 14, 4 * L + 1

        block = ctx.enter_context(nc.Block())

        @block.sync
        def _(sp):
            sp.dma_start(cs[:, 0, :], c.rearrange("b (p k) -> p (b k)", p=P)).then_inc(S["c_in"], 16)
            for t in range(TT):
                sp.dma_start(x_res[:, t, :], x[0, t * P:(t + 1) * P, :]).then_inc(S["x_in"], 16)
            win_in = w_in[0].rearrange("(p k) n -> p k n", k=KT)
            for n, (kind, what) in enumerate(plan):
                if n >= CH:
                    sp.wait_ge(S["chunk_done"], n - CH + 1)
                dst, arrived = chunk_at(n), chunk_in[n % CH]
                if kind == "mod":
                    l, v = mods[what // 2]
                    a = v * D + (what % 2) * HALF
                    sp.dma_start(dst, w_mod[l].rearrange("(p k) n -> p k n", k=KT)[:, :, a:a + HALF]).then_inc(arrived, 16)
                elif kind == "out":
                    sp.dma_start(dst, w_o[0].rearrange("(k p) n -> p k n", p=P)[:, :, what * HALF:(what + 1) * HALF]
                                 ).then_inc(arrived, 16)
                elif what == "kv":
                    sp.dma_start(dst[:, :, 0:LAT], win_in[:, :, KV0:KV0 + LAT]).then_inc(arrived, 16)
                    sp.dma_start(dst[:, :, LAT:LAT + 72], win_in[:, :, KI0:KI0 + 72]).then_inc(arrived, 16)
                else:
                    a = {"qi": QI0, "q": Q0, "v": V0, "u": U0}[what]
                    sp.dma_start(dst, win_in[:, :, a:a + HALF]).then_inc(arrived, 16)

            def expert(l, s, e):
                for w, src in enumerate((w_gate, w_up)):
                    sp.dma_start(gu_at(s)[:, w], src[l][bass.ds(e, 1)].rearrange("o (p k) f -> p (o k) f", k=KT)
                                 ).then_inc(gu_in[l][s], 16)
                sp.dma_start(dn_at(s), w_down[l][bass.ds(e, 1)].rearrange("o (p t) d -> p (o t) d", t=FT)
                             ).then_inc(dn_in[l][s], 16)

            groups = None
            for l in range(L):
                for j in range(XS):
                    if l == 0:
                        s = xslot(j)
                        last = max(n for n in range(len(plan)) if (n % CH) * 2 < 3 * s + 3 and (n % CH) * 2 + 2 > 3 * s)
                        sp.wait_ge(S["chunk_done"], last + 1)
                    else:
                        sp.wait_ge(E[l - 1]["down_done"], groups * XS - XS + 1 + j)
                    expert(l, xslot(j), j)
                sp.wait_ge(S["win_ready"], l + 1)
                groups = sp.value_load(grp_i[0:1, l:l + 1], min_val=0, max_val=NE // XS) + NE // XS
                with sp.Fori(1, groups) as i:
                    for b in range(XS):
                        e = sp.value_load(eid_i[0:1, bass.ds(i * XS + b, 1)], min_val=0, max_val=NE - 1)
                        sp.wait_ge(E[l]["down_done"], i * XS + (b - XS + 1))
                        expert(l, xslot(b), e)
            sp.wait_ge(S["out_ready"], TT)
            for t in range(TT):
                sp.dma_start(out[0, t * P:(t + 1) * P, :], xn[:, t, :]).then_inc(S["out_stored"], 16)
            sp.wait_ge(S["out_stored"], 16 * TT)

        @block.gpsimd
        def _(pool):
            own = 0

            def done(ins):
                nonlocal own
                own += 1
                ins.then_inc(S["pool_own"], 1)
                pool.wait_ge(S["pool_own"], own)

            done(pool.memset(ident[:], 0.0))
            done(pool.affine_select(out=ident[:], in_=ident[:], compare_op=ALU.not_equal, fill=1.0, base=0,
                                    pattern=[[-1, P]], channel_multiplier=1))
            done(pool.memset(mhalf[:], -0.5))
            done(pool.memset(ones[:], 1.0))
            pool.sem_inc(S["consts"], 1)
            for n, (dst, src) in enumerate(((bias_col[:, 0], b_mod[0].rearrange("(v p k) -> p v k", v=6, k=KT)),
                             (gain_col[:, 0], norm_mix[0].rearrange("(p k) -> p k", k=KT)),
                             (kvg[:], kv_norm[0].rearrange("(p o) -> p o", o=1)),
                             (wkv[:, 0, :], w_kv_up[0]),
                             (rows[0:1], b_mod[0:1, 2 * D:3 * D]), (rows[1:2], b_mod[0:1, 5 * D:6 * D]),
                             (rows[2:3], b_mod[1:2, 2 * D:3 * D]), (rows[3:4], b_mod[1:2, 5 * D:6 * D]),
                             (rows[4:5], pool_scale[0:1]), (rows[5:6], norm_out.rearrange("(o d) -> o d", o=1)),
                             (rows[6:7], norm_mix[1:2]), (rows[7:9], b_mod[1, 0:2 * D].rearrange("(v d) -> v d", v=2)),
                             (ws_raw, w_s[0].rearrange("g i j -> i g j")),
                             (bias_col[:, 1], b_mod[1].rearrange("(v p k) -> p v k", v=6, k=KT)),
                             (gain_col[:, 1], norm_ffn[0].rearrange("(p k) -> p k", k=KT)),
                             (gain_col[:, 2], norm_ffn[1].rearrange("(p k) -> p k", k=KT)),
                             (sgug[:], sgu_norm[0].rearrange("(g p) -> p g", p=P)),
                             (bsb, b_s[0].partition_broadcast(P)))):
                pool.dma_start(dst, src, allow_slow_non_contiguous=True).then_inc(S["early_in" if n < EARLY else "small_in"], 16)
            for l in range(L):
                for dst, src in ((wroute[:, l, :, 0:NG], w_gr[l].rearrange("(p k) n -> p k n", k=KT)),
                                 (wroute[:, l, :, NG:RCOLS], w_er[l].rearrange("(p k) n -> p k n", k=KT)),
                                 (broute[:, l, 0:NG], b_gr[l].partition_broadcast(P)),
                                 (broute[:, l, NG:RCOLS], b_er[l].partition_broadcast(P))):
                    pool.dma_start(dst, src).then_inc(S["late_in"], 16)
            pool.dma_start(wpool[:], w_pool[0].rearrange("g (t p) n -> p g t n", p=P)).then_inc(S["late_in"], 16)
            done(pool.memset(row_sel[:], 0.0))
            done(pool.affine_select(out=row_sel[:], in_=row_sel[:], compare_op=ALU.not_equal, fill=1.0, base=0,
                                    pattern=[[-1, 6], [0, P]], channel_multiplier=1))
            done(pool.memset(before[:], 1.0))
            done(pool.affine_select(out=before[:], in_=before[:], compare_op=ALU.is_gt, fill=0.0, base=0,
                                    pattern=[[1, P]], channel_multiplier=-1))
            done(pool.iota(slot_no[:], [[1, SLOTS]], base=0, channel_multiplier=0, allow_small_or_imprecise_dtypes=True))
            for t in range(TT):
                done(pool.iota(dist[:, t, :], [[-1, T]], base=t * P, channel_multiplier=1,
                               allow_small_or_imprecise_dtypes=True))
            done(pool.iota(edge[:], [[1, 16]], base=1, channel_multiplier=0, allow_small_or_imprecise_dtypes=True))
            done(pool.iota(rank[:], [[-1, 8]], base=8, channel_multiplier=0, allow_small_or_imprecise_dtypes=True))
            done(pool.iota(eid_i[:], [[0, 2], [1, NE]], base=0, channel_multiplier=0))
            pool.sem_inc(S["consts"], 1)

            def power(n):
                pool.wait_ge(S["mean_sq"], n + 1)
                pool.tensor_tensor(stat[:, 4:6], stat[:, 2:4], mhalf[:], ALU.pow).then_inc(S["inv_rms"], 1)

            power(0)
            pool.wait_ge(S["kv_ms"], 1)
            pool.tensor_tensor(stat[:, 10:12], stat[:, 8:10], mhalf[:], ALU.pow).then_inc(S["kv_inv"], 1)
            pool.wait_ge(S["ln_ms"], 1)
            pool.tensor_tensor(stat[:, 18:20], stat[:, 16:18], mhalf[:], ALU.pow).then_inc(S["ln_inv"], 1)
            for n in range(1, 5):
                power(n)

        @block.tensor
        def _(pe):
            def arrived(key):
                n = chunk_no[key]
                pe.wait_ge(chunk_in[n % CH], arrivals(n))
                return chunk_at(n)

            def turned(src, t, k, natural):
                return src[:, t, k * P:(k + 1) * P] if natural else src[:, t, :].rearrange("p (q k) -> p k q", k=KT)[:, k]

            def mod_chunk(m):
                vec, half = mods[m // 2], m % 2
                w = arrived(("mod", m))
                if m >= 2:
                    pe.wait_ge(S["mod_kept"], m - 1)
                    before_it = mods[(m - 2) // 2]
                    if m % 2 and before_it in columns:
                        pe.wait_ge(S["col_kept"], columns.index(before_it) + 1)
                if m == 7:
                    pe.wait_ge(S["pT_ready"], 6)
                wide = vec in GATE
                o = bank[m % 2][:, :] if wide else bank[m % 2][0:1, :]
                if vec in ROW_BIAS:
                    r = ROW_BIAS[vec]
                    pe.matmul(o, row_sel[:, r, :] if wide else ident[0:9, r:r + 1],
                              rows[:, half * HALF:(half + 1) * HALF], start=True, stop=False)
                for k in range(KT):
                    ins = pe.matmul(o, csb[:, k, :] if wide else cs[:, 2, k:k + 1], w[:, k, :],
                                    start=(k == 0 and vec not in ROW_BIAS), stop=(k == KT - 1))
                ins.then_inc(S["chunk_done"], 1)

            def column(v):
                vec = columns[v]
                pe.wait_ge(S["mod_kept"], 2 * mods.index(vec) + 2)
                for k in range(KT):
                    src = turned(gates[0:1, 3:4, :], 0, k, natural=vec in ((1, 0), (1, 1)))
                    ins = pe.matmul(bank[1][:, k:k + 1], src, ones[0:1, 0:1], start=True, stop=True)
                ins.then_inc(S["col_done"], 1)

            def mod_run(ms):
                waiting = None
                for m in ms:
                    mod_chunk(m)
                    if waiting is not None:
                        column(waiting)
                        waiting = None
                    if m % 2 and mods[m // 2] in columns:
                        waiting = columns.index(mods[m // 2])
                if waiting is not None:
                    column(waiting)

            def turn(n, natural=False):
                pe.wait_ge(S["xn_ready"], n + 1)
                for kk in range(4):
                    for k in (2 * kk, 2 * kk + 1):
                        for t in range(TT):
                            a = (k % 2) * T + t * P
                            ins = pe.transpose(bank[2 + kk][:, a:a + P], turned(xn, t, k, natural), ident[:])
                    ins.then_inc(S["xT_done"], 1)

            def hT_ready(n):
                pe.wait_ge(S["hT_act"], 4 * n)
                pe.wait_ge(S["hT_dve"], 4 * n)

            def by_channel(key, banks, first_done):
                w = arrived(key)
                for m in range(4):
                    for k in range(KT):
                        ins = pe.matmul(bank[banks[m // 2]][:, (m % 2) * T:(m % 2 + 1) * T], w[:, k, m * P:(m + 1) * P],
                                        hT[:, k, :], start=(k == 0), stop=(k == KT - 1))
                    if m == 1:
                        ins.then_inc(first_done, 1)
                ins.then_inc(S["chunk_done"], 1)

            pe.wait_ge(S["consts"], 1)
            turn(0)
            pe.wait_ge(S["csb_ready"], 1)
            mod_run(range(0, 4))
            hT_ready(1)
            by_channel(("in", "qi"), (6, 7), S["qi_done"])
            w = arrived(("in", "kv"))
            for t in range(TT):
                for k in range(KT):
                    ins = pe.matmul(bank[2][:, t * 200:(t + 1) * 200], hT[:, k, t * P:(t + 1) * P], w[:, k, 0:200],
                                    start=(k == 0), stop=(k == KT - 1))
            ins.then_inc(S["chunk_done"], 1)
            pe.wait_ge(S["kv_ready"], 1)
            for t in range(TT):
                pe.transpose(bank[5][:, t * P:(t + 1) * P], kidup[:, t, :], ident[:])
            for t in range(TT):
                ins = pe.transpose(bank[5][:, T + t * P:T + (t + 1) * P], kvn[:, t, :], ident[:])
            ins.then_inc(S["kt_turned"], 1)

            def head_units(lhs, rhs, banks, done, consumed):
                for u in range(6):
                    t, per = (0, 4) if u < 2 else (1, 2)
                    h0, span = (4 * u, P) if t == 0 else (2 * (u - 2), T)
                    if u >= 3:
                        pe.wait_ge(consumed, u - 2)
                    for i in range(per):
                        r, k = divmod(h0 + i, 4)
                        r *= HD
                        ins = pe.matmul(bank[banks[u % 3]][:, i * span:(i + 1) * span],
                                        lhs[r:r + HD, k, t * P:(t + 1) * P], rhs[r:r + HD, 0:span],
                                        start=True, stop=True)
                    ins.then_inc(done, 1)

            pe.wait_ge(S["kiT_ready"], 1)
            pe.wait_ge(S["qi_kept"], 2)
            head_units(qiT, kiT, (3, 4, 6), S["score_done"], S["score_relu"])
            pe.wait_ge(S["small_in"], 16 * SMALL)
            pe.wait_ge(S["consts"], 2)
            for g in range(4):
                ins = pe.transpose(bank[7][:, g * P:(g + 1) * P], ws_raw[:, g, :], ident[:])
            ins.then_inc(S["ws_turned"], 1)
            for k in range(KT):
                ins = pe.matmul(bank[2][:, k:k + 1], rows[:, k * P:(k + 1) * P], ident[0:9, 6:7], start=True, stop=True)
            ins.then_inc(S["gain_row"], 1)
            pe.wait_ge(S["kvnT_ready"], 1)
            pe.wait_ge(S["wsT_copied"], 1)
            by_channel(("in", "q"), (5, 7), S["q_done"])
            pe.wait_ge(S["score_relu"], 5)
            w = arrived(("in", "v"))
            for t in range(TT):
                for k in range(KT):
                    ins = pe.matmul(bank[3 + t][:, :], hT[:, k, t * P:(t + 1) * P], w[:, k, :],
                                    start=(k == 0), stop=(k == KT - 1))
                ins.then_inc(S["v_done"] if t == 0 else S["chunk_done"], 1)
            pe.wait_ge(S["gain_ready"], 1)
            pe.wait_ge(S["wkv_ready"], 1)
            pe.matmul(bank[2][:, 0:T], wkv[:, 1, :], kvnT, start=True, stop=True)
            for t in range(TT):
                ins = pe.matmul(bank[2][:, T + t * P:T + (t + 1) * P], kvnT[:, t * P:(t + 1) * P], wkv[:, 2, :],
                                start=True, stop=True)
            ins.then_inc(S["kup_done"], 1)
            pe.wait_ge(S["score_relu"], 6)
            pe.wait_ge(S["q_kept"], 1)
            by_channel(("in", "u"), (6, 5), S["u_done"])
            mod_run(range(4, 6))
            pe.wait_ge(S["vln_ready"], 1)
            pe.wait_ge(S["wsT_ready"], 1)
            for t in range(TT):
                for g in range(4):
                    a = (g % 2) * T + t * P
                    ins = pe.matmul(bank[3 + g // 2][:, a:a + P], vtk[:, t, g * P:(g + 1) * P], wsT[:, g, :],
                                    start=True, stop=True)
            ins.then_inc(S["sgu_done"], 1)
            pe.wait_ge(S["q_kept"], 2)
            pe.wait_ge(S["kup_kept"], 1)
            pe.wait_ge(S["u_kept"], 2)
            head_units(qT, kT, (6, 7, 2), S["att_done"], S["att_shift"])

            def turn_p(v):
                pe.wait_ge(S["att_ready"], v + 1)
                if v >= 2:
                    pe.wait_ge(S["pT_ready"], v - 1)
                b = bank[(5, 1)[v % 2]]
                for i in range(4):
                    src = att0[:, 4 * v + i, :] if v < 2 else att1[:, 2 * (v - 2) + i % 2, (i // 2) * P:(i // 2 + 1) * P]
                    ins = pe.transpose(b[:, i * P:(i + 1) * P], src, ident[:])
                ins.then_inc(S["p_turned"], 1)

            def values(t):
                for b in range(2):
                    for s in range(t + 1):
                        rhs = pT0[:, b * 512:(b + 1) * 512] if t == 0 else pT1[:, s, b * 512:(b + 1) * 512]
                        ins = pe.matmul(bank[3 + b][:, :], v2[:, s, :], rhs, start=(s == 0), stop=(s == t))
                    ins.then_inc(S["pv_done"], 1)

            pe.wait_ge(S["mod_kept"], 6)
            turn_p(0)
            turn_p(1)
            pe.wait_ge(S["pT_ready"], 2)
            pe.wait_ge(S["bT_ready"], 1)
            values(0)
            for v in range(2, 6):
                turn_p(v)
            pe.wait_ge(S["pT_ready"], 6)
            pe.wait_ge(S["cat_act"], 1)
            pe.wait_ge(S["cat_dve"], 1)
            values(1)
            pe.wait_ge(S["cat_act"], 2)
            pe.wait_ge(S["cat_dve"], 2)
            pe.wait_ge(S["att_shift"], 6)
            for half in range(2):
                w = arrived(("out", half))
                for t in range(TT):
                    for k in range(KT):
                        ins = pe.matmul(bank[(3, 4, 6, 7)[2 * half + t]][:, :], catT[:, k, t * P:(t + 1) * P], w[:, k, :],
                                        start=(k == 0), stop=(k == KT - 1))
                    ins.then_inc(S["mix_done"] if t == 0 else S["chunk_done"], 1)
            mod_run(range(6, 12))

            def route(l):
                turn(2 * l + 1)
                hT_ready(2 * l + 2)
                pe.wait_ge(S["late_in"], 16 * LATE)
                for t in range(TT):
                    for k in range(KT):
                        ins = pe.matmul(bank[6][:, t * 64:t * 64 + RCOLS], hT[:, k, t * P:(t + 1) * P], wroute[:, l, k, :],
                                        start=(k == 0), stop=(k == KT - 1))
                ins.then_inc(S["lg_done"], 1)
                if l == 0:
                    mod_run(range(12, 16))
                pe.wait_ge(S["asg_ready"], l + 1)
                b, a0, a1 = bank[7], asg[:, 0, :], asg[:, 1, :]
                pe.matmul(b[:, 0:NE], before[:], a0, start=True, stop=True)
                pe.matmul(b[:, NE:2 * NE], ones[:], a0, start=True, stop=False)
                pe.matmul(b[:, NE:2 * NE], before[:], a1, start=False, stop=True)
                pe.matmul(b[:, 224:224 + NE], ones[:], a0, start=True, stop=False)
                pe.matmul(b[:, 224:224 + NE], ones[:], a1, start=False, stop=True)
                pe.matmul(b[0:NE, 64:64 + P], a0, ones[:], start=True, stop=False)
                pe.matmul(b[0:NE, 64:64 + P], a1, ones[:], start=False, stop=True).then_inc(S["tot_done"], 1)
                pe.wait_ge(S["tot_ready"], l + 1)
                pe.matmul(b[:, 192:192 + NE], tot[0:NE, :], before[0:NE, 0:NE], start=True, stop=True).then_inc(S["off_done"], 1)
                if l == 0:
                    mod_run(range(16, 20))
                pe.wait_ge(S["sel_ready"], l + 1)
                for k in range(KT):
                    if k >= 4:
                        pe.wait_ge(S["xg_dve" if k % 2 else "xg_act"], 4 * l + (k - 4) // 2 + 1)
                    for t in range(TT):
                        ins = pe.matmul(bank[2 + k % 4][:, :], turned(xn, t, k, False), sel[:, t, :],
                                        start=(t == 0), stop=(t == TT - 1))
                    ins.then_inc(S["xg_done"], 1)
                pe.wait_ge(S["comb_ready"], l + 1)
                for s in range(4):
                    for t in range(TT):
                        a = (s % 2) * T + t * P
                        ins = pe.transpose(bank[6 + s // 2][:, a:a + P], comb[:, t, s * P:(s + 1) * P], ident[:])
                    if s % 2:
                        ins.then_inc(S["comb_turned"], 1)
                if l == 0:
                    mod_run(range(20, 24))
                    pe.wait_ge(S["xg_act"], 4)
                    for half in range(2):
                        ins = pe.matmul(bank[2 + 2 * half][:, :], row_sel[:, 4, :], rows[:, half * HALF:(half + 1) * HALF],
                                        start=True, stop=True)
                    ins.then_inc(S["row_done"], 1)
                    pe.wait_ge(S["row_kept"], 1)
                pe.wait_ge(S["combT_ready"], 2 * l + 2)

            def experts(l):
                e = E[l]

                def gate_up(j, b, i, part):
                    if part == 0:
                        s = xslot(b)
                        pe.wait_ge(e["xw_ready"], j + 1)
                        pe.wait_ge(gu_in[l][s], 32 * (i + 1))
                        if not isinstance(j, int) or j >= 2:
                            pe.wait_ge(e["act_ready"], j - 1)
                    w = gu_at(xslot(b))
                    for k in range(4 * part, 4 * part + 4):
                        ins = pe.matmul(bank[b % 2][:, :].rearrange("p (w f) -> p w f", w=2), xw[:, b % 2, k, :], w[:, :, k, :],
                                        start=(k == 0), stop=(k == KT - 1))
                    if part == 1:
                        ins.then_inc(e["gu_done"], 1)

                def turn_act(j, b):
                    pe.wait_ge(e["act_ready"], j + 1)
                    for t in range(FT):
                        ins = pe.transpose(bank[2 + b % 2][:, t * P:(t + 1) * P], act_s[:, b % 2, t, :], ident[:])
                    ins.then_inc(e["act_turned"], 1)

                def down(j, b, i):
                    s = xslot(b)
                    pe.wait_ge(dn_in[l][s], 16 * (i + 1))
                    pe.wait_ge(e["actT_ready"], j + 1)
                    if not isinstance(j, int) or j >= 2:
                        pe.wait_ge(e["y_act"], j - 1)
                        pe.wait_ge(e["y_dve"], j - 1)
                    for k in range(KT):
                        for t in range(FT):
                            ins = pe.matmul(bank[4 + 2 * (b % 2) + k // 4][:, (k % 4) * WIN:(k % 4 + 1) * WIN],
                                            dn_at(s)[:, t, k * P:(k + 1) * P], actT[:, b % 2, t, :],
                                            start=(t == 0), stop=(t == FT - 1))
                    ins.then_inc(e["down_done"], 1)

                def group(i):
                    for b in range(XS):
                        j = i * XS + b
                        first = isinstance(i, int) and j == 0
                        gate_up(j, b, i, 0)
                        if not first:
                            turn_act(i * XS + (b - 1), (b - 1) % XS)
                        gate_up(j, b, i, 1)
                        if not first:
                            down(i * XS + (b - 1), (b - 1) % XS, i if b else i - 1)

                pe.wait_ge(S["win_ready"], l + 1)
                groups = pe.value_load(grp_i[0:1, l:l + 1], min_val=0, max_val=NE // XS) + NE // XS
                pe.wait_ge(S["mod_kept"], 24)
                group(0)
                with pe.Fori(1, groups) as i:
                    group(i)
                turn_act(groups * XS - 1, XS - 1)
                down(groups * XS - 1, XS - 1, groups - 1)

            def combine(l):
                pe.wait_ge(E[l]["y_last_act"], 1)
                pe.wait_ge(E[l]["y_last_dve"], 1)
                for s in range(4):
                    for half in range(2):
                        if s >= 2:
                            pe.wait_ge(S["ysl_dve" if half else "ysl_act"], 4 * l + s - 1)
                        for k in range(4):
                            ins = pe.transpose(bank[2 * (s % 2) + half][:, k * P:(k + 1) * P],
                                               yT[:, 4 * half + k, s * P:(s + 1) * P], ident[:])
                        ins.then_inc(S["y_turned"], 1)
                for s in range(4):
                    pe.wait_ge(S["ysl_act"], 4 * l + s + 1)
                    pe.wait_ge(S["ysl_dve"], 4 * l + s + 1)
                    for half in range(2):
                        for t in range(TT):
                            ins = pe.matmul(bank[4 + 2 * half + t][:, :], combT[:, s, t * P:(t + 1) * P],
                                            ysl[:, s, half * HALF:(half + 1) * HALF], start=(s == 0), stop=(s == 3))
                            if s == 3:
                                ins.then_inc(S["mix_done"], 1)

            route(0)
            experts(0)
            combine(0)
            turn(2, natural=True)
            for g in range(4):
                pe.wait_ge(S["pool_ready"], g + 1)
                for t in range(TT):
                    for i in range(2):
                        ins = pe.matmul(bank[4 + 2 * (g // 2) + t][:, (g % 2) * 256:(g % 2 + 1) * 256],
                                        hT[:, 2 * g + i, t * P:(t + 1) * P], wpool[:, g, i, :], start=(i == 0), stop=(i == 1))
                    if g % 2:
                        ins.then_inc(S["mix_done"], 1)
            route(1)
            experts(1)
            combine(1)
            for half in range(2):
                ins = pe.matmul(bank[2 + half][:, :], row_sel[:, 5, :], rows[:, half * HALF:(half + 1) * HALF],
                                start=True, stop=True)
            ins.then_inc(S["row_done"], 1)

        @block.scalar
        def _(act):
            def mod_run(ms):
                for m in ms:
                    vec, half = mods[m // 2], m % 2
                    act.wait_ge(S["chunk_done"], chunk_no["mod", m] + 1)
                    at = slice(half * HALF, (half + 1) * HALF)
                    if vec in GATE:
                        act.copy(gates[:, GATE[vec], at], bank[m % 2][:, :]).then_inc(S["mod_kept"], 1)
                    else:
                        act.copy(gates[0:1, 3, at], bank[m % 2][0:1, :]).then_inc(S["mod_kept"], 1)
                        if half:
                            v = columns.index(vec)
                            act.wait_ge(S["col_done"], v + 1)
                            act.copy(raw_col[:, v, :], bank[1][:, 0:KT]).then_inc(S["col_kept"], 1)

            def squares(n):
                if n == 0:
                    act.wait_ge(S["x_in"], 16 * TT)
                else:
                    act.wait_ge(S["x_ready"], n)
                for t in range(TT):
                    ins = act.activation(xn[:, t, :], x_res[:, t, :], ACT.Square, accum_out=stat[:, t:t + 1])
                ins.then_inc(S["square_sum"], 1)

            def modulated(n, l, which, dst):
                act.wait_ge(S["ab_ready"], n + 1)
                for k in range(4):
                    act.wait_ge(S["xT_done"], 4 * n + k // 2 + 1)
                    act.activation(dst[:, k, :], bank[2 + k // 2][:, (k % 2) * T:(k % 2 + 1) * T], ACT.Identity,
                                   scale=ab[:, l, which, k:k + 1], bias=ab[:, l, which + 1, k:k + 1]).then_inc(S["hT_act"], 1)

            act.wait_ge(S["c_in"], 16)
            act.activation(cs[:, 1, :], cs[:, 0, :], ACT.Tanh, scale=0.5).then_inc(S["c_tanh"], 1)
            squares(0)
            mod_run(range(0, 4))
            modulated(0, 0, 0, hT)
            flat = lambda v: v.rearrange("p a b -> p (a b)")
            for i, ready in enumerate((S["qi_done"], None)):
                if ready is not None:
                    act.wait_ge(ready, 1)
                else:
                    act.wait_ge(S["chunk_done"], chunk_no["in", "qi"] + 1)
                act.copy(flat(qiT[:, 2 * i:2 * i + 2, :]), bank[6 + i][:, :]).then_inc(S["qi_kept"], 1)
            act.wait_ge(S["chunk_done"], chunk_no["in", "kv"] + 1)
            for t in range(TT):
                ins = act.activation(kvn[:, t, :], bank[2][:, t * 200:t * 200 + LAT], ACT.Square, accum_out=stat[:, 6 + t:7 + t])
            ins.then_inc(S["kv_sq"], 1)
            act.wait_ge(S["early_in"], 16 * EARLY)
            for w in range(2):
                for i in range(2):
                    ins = act.copy(wkv[:, 1 + w, i * HD:(i + 1) * HD], wkv[:, 0, w * HD:(w + 1) * HD])
            ins.then_inc(S["wkv_ready"], 1)
            for u in range(6):
                act.wait_ge(S["score_done"], u + 1)
                if u >= 2:
                    act.wait_ge(S["score_added"], u - 1)
                act.activation(relu[:, u % 2, :], bank[(3, 4, 6)[u % 3]][:, :], ACT.Relu, scale=HD ** -0.5
                               ).then_inc(S["score_relu"], 1)
            act.wait_ge(S["ws_turned"], 1)
            act.copy(flat(wsT), bank[7][:, :]).then_inc(S["wsT_copied"], 1)
            for i, b in enumerate((5, 7)):
                if i == 0:
                    act.wait_ge(S["q_done"], 1)
                else:
                    act.wait_ge(S["chunk_done"], chunk_no["in", "q"] + 1)
                act.copy(flat(qT[:, 2 * i:2 * i + 2, :]), bank[b][:, :]).then_inc(S["q_kept"], 1)
            for t in range(TT):
                if t == 0:
                    act.wait_ge(S["v_done"], 1)
                else:
                    act.wait_ge(S["chunk_done"], chunk_no["in", "v"] + 1)
                act.copy(vtk[:, t, :], bank[3 + t][:, :])
                act.activation(gtmp[:, t, :], bank[3 + t][:, :], ACT.Square).then_inc(S["v_kept"], 1)
            act.wait_ge(S["kup_done"], 1)
            act.copy(arena[:, 11008:11520], bank[2][:, :]).then_inc(S["kup_kept"], 1)
            act.wait_ge(S["v_poly"], 1)
            act.activation(flat(gtmp), flat(gtmp), ACT.Tanh, scale=GELU_C).then_inc(S["v_tanh"], 1)
            act.wait_ge(S["ws_turned"], 1)
            act.wait_ge(S["score_done"], 6)
            for i, b in enumerate((6, 5)):
                if i == 0:
                    act.wait_ge(S["u_done"], 1)
                else:
                    act.wait_ge(S["chunk_done"], chunk_no["in", "u"] + 1)
                act.copy(flat(uT[:, 2 * i:2 * i + 2, :]), bank[b][:, :])
                act.activation(flat(usq[:, 2 * i:2 * i + 2, :]), bank[b][:, :], ACT.Square).then_inc(S["u_kept"], 1)
            act.wait_ge(S["u_poly"], 1)
            act.activation(flat(usq), flat(usq), ACT.Tanh, scale=GELU_C).then_inc(S["u_tanh"], 1)
            mod_run(range(4, 6))

            def exps(u):
                act.wait_ge(S["att_shift"], u + 1)
                t, heads = (0, range(4 * u, 4 * u + 4)) if u < 2 else (1, range(2 * u - 4, 2 * u - 2))
                for h in heads:
                    a = att0[:, h, :] if t == 0 else att1[:, h, :]
                    ins = act.activation(a, a, ACT.Exp, scale=HD ** -0.5, bias=amax[:, t, h:h + 1], accum_out=asum[:, t, h:h + 1])
                ins.then_inc(S["att_exp"], 1)

            def keep_p(v):
                act.wait_ge(S["p_turned"], v + 1)
                if v == 0:
                    act.wait_ge(S["u_ready"], 1)
                if v == 2:
                    act.wait_ge(S["pv_done"], 2)
                b = bank[(5, 1)[v % 2]]
                if v < 2:
                    act.copy(pT0[:, v * 512:(v + 1) * 512], b[:, :]).then_inc(S["pT_ready"], 1)
                else:
                    a = 2 * (v - 2) * P
                    act.copy(pT1[:, :, a:a + 2 * P], b[:, :].rearrange("p (s q) -> p s q", s=2)).then_inc(S["pT_ready"], 1)

            def keep_heads(t):
                act.wait_ge(S["pv_done"], 2 * t + 1)
                act.copy(catT[0:HD, 0:4, t * P:(t + 1) * P], bank[3][0:HD, :].rearrange("p (k q) -> p k q", k=4)
                         ).then_inc(S["cat_act"], 1)

            exps(0), exps(1), keep_p(0), keep_p(1), exps(2), keep_heads(0), exps(3), keep_p(2)
            exps(4), keep_p(3), exps(5), keep_p(4), keep_p(5), keep_heads(1)
            mod_run(range(6, 12))

            def route(l):
                squares(2 * l + 1)
                modulated(2 * l + 1, l, 2, hT)
                act.wait_ge(S["g_shift"], l + 1)
                act.activation(rt_ge, rt_gd, ACT.Exp).then_inc(S["e_group"], 1)
                act.wait_ge(S["e_pair_in"], l + 1)
                act.activation(rt_q, rt_dd, ACT.Exp).then_inc(S["e_pair"], 1)
                if l == 0:
                    mod_run(range(12, 20))
                for k in range(0, KT, 2):
                    act.wait_ge(S["xg_done"], KT * l + k + 1)
                    act.activation(xgT[:, k, 0:SLOTS], bank[2 + k % 4][:, :], ACT.Identity,
                                   scale=ab[:, l, 2, k:k + 1], bias=ab[:, l, 3, k:k + 1]).then_inc(S["xg_act"], 1)
                for i in range(2):
                    act.wait_ge(S["comb_turned"], 2 * l + i + 1)
                    act.copy(flat(combT[:, 2 * i:2 * i + 2, :]), bank[6 + i][:, :]).then_inc(S["combT_ready"], 1)
                if l == 0:
                    mod_run(range(20, 24))

            def experts(l):
                e = E[l]

                def tanh(j, b):
                    act.wait_ge(e["gu_done"], j + 1)
                    if not isinstance(j, int) or j >= 2:
                        act.wait_ge(e["act_ready"], j - 1)
                    act.activation(th[:, b % 2, :], bank[b % 2][:, 0:FE], ACT.Tanh, scale=0.5).then_inc(e["gu_tanh"], 1)

                def keep_act(j, b):
                    act.wait_ge(e["act_turned"], j + 1)
                    if not isinstance(j, int) or j >= 2:
                        act.wait_ge(e["down_done"], j - 1)
                    act.copy(flat(actT[:, b % 2]), bank[2 + b % 2][:, 0:FT * P]).then_inc(e["actT_ready"], 1)

                def keep_y(j, b, signal):
                    start = act.value_load(win_i[0:1, bass.ds(j, 1)], min_val=0, max_val=SLOTS)
                    act.wait_ge(e["down_done"], j + 1)
                    if not isinstance(j, int) or j >= 1:
                        act.wait_ge(e["y_act"], j)
                    act.copy(yT[:, 0:4, bass.ds(start, WIN)], bank[4 + 2 * (b % 2)][:, :].rearrange("p (k s) -> p k s", k=4)
                             ).then_inc(signal, 1)

                def group(i):
                    for b in range(XS):
                        first = isinstance(i, int) and i * XS + b == 0
                        if not first:
                            keep_act(i * XS + (b - 1), (b - 1) % XS)
                        tanh(i * XS + b, b)
                        if not first:
                            keep_y(i * XS + (b - 1), (b - 1) % XS, e["y_act"])

                act.wait_ge(S["win_ready"], l + 1)
                groups = act.value_load(grp_i[0:1, l:l + 1], min_val=0, max_val=NE // XS) + NE // XS
                group(0)
                with act.Fori(1, groups) as i:
                    group(i)
                keep_act(groups * XS - 1, XS - 1)
                keep_y(groups * XS - 1, XS - 1, e["y_last_act"])

            def combine(l):
                for s in range(4):
                    act.wait_ge(S["y_turned"], 8 * l + 2 * s + 1)
                    act.copy(ysl[:, s, 0:HALF], bank[2 * (s % 2)][:, :]).then_inc(S["ysl_act"], 1)

            route(0)
            experts(0)
            combine(0)
            squares(2)
            modulated(2, 1, 0, hp[:, :, PAD:PAD + T])
            route(1)
            experts(1)
            combine(1)
            squares(4)

        @block.vector
        def _(dve):
            own = 0

            def done(ins):
                nonlocal own
                own += 1
                ins.then_inc(S["dve_own"], 1)
                dve.wait_ge(S["dve_own"], own)

            tt, ts, stt = dve.tensor_tensor, dve.tensor_scalar, dve.scalar_tensor_tensor

            def normed(n, write=True):
                dve.wait_ge(S["square_sum"], n + 1)
                ts(stat[:, 2:4], stat[:, 0:2], 1.0 / D, EPS, ALU.mult, ALU.add).then_inc(S["mean_sq"], 1)
                dve.wait_ge(S["inv_rms"], n + 1)
                if write:
                    for t in range(TT):
                        ins = ts(xn[:, t, :], x_res[:, t, :], stat[:, 4 + t:5 + t], None, ALU.mult)
                    ins.then_inc(S["xn_ready"], 1)

            def scale_shift(n, l, which):
                sh, sc = (l, which // 2 * 3), (l, which // 2 * 3 + 1)
                dve.wait_ge(S["col_kept"], columns.index(sc) + 1)
                a, s = raw_col[:, columns.index(sc), :], raw_col[:, columns.index(sh), :]
                if sh in ROW_BIAS:
                    done(dve.tensor_copy(ab[:, l, which + 1, :], s))
                    done(ts(ab[:, l, which, :], a, 1.0, None, ALU.add))
                else:
                    done(tt(ab[:, l, which + 1, :], s, bias_col[:, l, sh[1], :], ALU.add))
                    done(stt(ab[:, l, which, :], a, 1.0, bias_col[:, l, sc[1], :], ALU.add, ALU.add))
                g = {(0, 0): 0, (0, 2): 1, (1, 2): 2, (1, 0): 3}[l, which]
                tt(ab[:, l, which, :], ab[:, l, which, :], gain_col[:, g, :], ALU.mult).then_inc(S["ab_ready"], 1)
                dve.wait_ge(S["ab_ready"], n + 1)

            def modulated(n, l, which, dst):
                for k in range(4, KT):
                    dve.wait_ge(S["xT_done"], 4 * n + k // 2 + 1)
                    ts(dst[:, k, :], bank[2 + k // 2][:, (k % 2) * T:(k % 2 + 1) * T], ab[:, l, which, k:k + 1],
                       ab[:, l, which + 1, k:k + 1], ALU.mult, ALU.add).then_inc(S["hT_dve"], 1)

            def residual(gate, parts, tmp):
                for n, (t, half, b, ready, value) in enumerate(parts):
                    dve.wait_ge(ready, value)
                    at = slice(half * HALF, (half + 1) * HALF)
                    y = tmp[:, (n % 2) * HALF:(n % 2 + 1) * HALF]
                    done(tt(y, bank[b][:, :], gates[:, gate, at], ALU.mult))
                    ins = tt(x_res[:, t, at], x_res[:, t, at], y, ALU.add)
                    if n < 3:
                        done(ins)
                ins.then_inc(S["x_ready"], 1)
                dve.wait_ge(S["x_ready"], {0: 1, 1: 2, 2: 3, 3: 4}[gate])

            dve.wait_ge(S["c_tanh"], 1)
            done(stt(cs[:, 1, :], cs[:, 1, :], 1.0, cs[:, 0, :], ALU.add, ALU.mult))
            done(ts(cs[:, 2, :], cs[:, 1, :], 0.5, None, ALU.mult))
            dve.tensor_copy(csb, cs[:, 2, :].unsqueeze(2).to_broadcast([P, KT, P])).then_inc(S["csb_ready"], 1)
            normed(0)
            dve.wait_ge(S["early_in"], 16 * EARLY)
            scale_shift(0, 0, 0)
            modulated(0, 0, 0, hT)

            dve.wait_ge(S["kv_sq"], 1)
            ts(stat[:, 8:10], stat[:, 6:8], 1.0 / LAT, EPS, ALU.mult, ALU.add).then_inc(S["kv_ms"], 1)
            for t in range(TT):
                a = t * 200 + LAT
                dve.tensor_copy(kidup[:, t, :].rearrange("p (r d) -> p r d", r=2),
                                bank[2][:, a:a + HD].unsqueeze(1).to_broadcast([P, 2, HD]))
                ts(w8[:, t, :], bank[2][:, a + HD:a + HD + H], H ** -0.5, None, ALU.mult)
            dve.wait_ge(S["kv_inv"], 1)
            for t in range(TT):
                ins = ts(kvn[:, t, :], bank[2][:, t * 200:t * 200 + LAT], stat[:, 10 + t:11 + t], None, ALU.mult)
            ins.then_inc(S["kv_ready"], 1)
            dve.wait_ge(S["kt_turned"], 1)
            dve.tensor_copy(kiT, bank[5][:, 0:T]).then_inc(S["kiT_ready"], 1)
            ts(kvnT, bank[5][:, T:2 * T], kvg[:, 0:1], None, ALU.mult).then_inc(S["kvnT_ready"], 1)

            dve.wait_ge(S["kv_ready"], 1)
            for u in range(6):
                t, per, h0 = (0, 4, 4 * u) if u < 2 else (1, 2, 2 * (u - 2))
                span = P if t == 0 else T
                dve.wait_ge(S["score_relu"], u + 1)
                for i in range(per):
                    h, r = h0 + i, relu[:, u % 2, i * span:(i + 1) * span]
                    s, w = score[:, t, 0:span], w8[:, t, head_at(h):head_at(h) + 1]
                    if h == 0:
                        ins = ts(s, r, w, None, ALU.mult)
                    else:
                        ins = stt(s, r, w, s, ALU.mult, ALU.add)
                    if i < per - 1:
                        done(ins)
                ins.then_inc(S["score_added"], 1)
                dve.wait_ge(S["score_added"], u + 1)
            for t in range(TT):
                done(dve.memset(score[0:CHUNK, t, (t + 1) * P - CHUNK:(t + 1) * P], NEVER))

            def gelu_poly(sq, v, after):
                done(ts(sq, sq, GELU_A, 1.0, ALU.mult, ALU.add))
                tt(sq, sq, v, ALU.mult).then_inc(after, 1)

            flat = lambda v: v.rearrange("p a b -> p (a b)")

            def select(t):
                s = score[:, t, 0:(t + 1) * P]
                for r in range(TOPK // 8):
                    done(dve.max(best[:], s))
                    done(dve.match_replace(s, best[:], s, TAKEN))
                done(ts(keep[:, t, 0:(t + 1) * P], s, TAKEN, FAR, ALU.not_equal, ALU.mult))

            select(0)
            dve.wait_ge(S["v_kept"], 2)
            gelu_poly(flat(gtmp), flat(vtk), S["v_poly"])
            select(1)
            dve.wait_ge(S["gain_row"], 1)
            dve.tensor_copy(gain_col[:, 3, :], bank[2][:, 0:KT]).then_inc(S["gain_ready"], 1)
            dve.wait_ge(S["wsT_copied"], 1)
            dve.memset(wsT[CHUNK:P, :, 0:CHUNK], 0.0).then_inc(S["wsT_ready"], 1)
            dve.wait_ge(S["consts"], 2)
            done(stt(flat(dist), flat(dist), -1.0, flat(dist), ALU.mult, ALU.max))
            dve.wait_ge(S["v_tanh"], 1)
            done(stt(flat(vtk), flat(gtmp), 1.0, flat(vtk), ALU.add, ALU.mult))
            for t in range(TT):
                done(dve.bn_stats(rt[:, 660 + 6 * t:666 + 6 * t], vtk[:, t, :]))
                done(dve.bn_aggr(rt[:, 680 + 2 * t:682 + 2 * t], rt[:, 660 + 6 * t:666 + 6 * t]))
                ins = ts(stat[:, 16 + t:17 + t], rt[:, 681 + 2 * t:682 + 2 * t], 0.25, EPS, ALU.mult, ALU.add)
            ins.then_inc(S["ln_ms"], 1)
            dve.wait_ge(S["ln_inv"], 1)
            done(ts(stat[:, 18:20], stat[:, 18:20], 0.5, None, ALU.mult))
            for t in range(TT):
                ins = ts(vtk[:, t, :], vtk[:, t, :], rt[:, 680 + 2 * t:681 + 2 * t], stat[:, 18 + t:19 + t],
                         ALU.subtract, ALU.mult)
            ins.then_inc(S["vln_ready"], 1)
            dve.wait_ge(S["u_kept"], 2)
            gelu_poly(flat(usq), flat(uT), S["u_poly"])

            def shift(u):
                dve.wait_ge(S["att_done"], u + 1)
                t, heads = (0, range(4 * u, 4 * u + 4)) if u < 2 else (1, range(2 * u - 4, 2 * u - 2))
                span, b = (P, T)[t], bank[(6, 7, 2)[u % 3]]
                views = [(att0 if t == 0 else att1)[:, h, 0:span] for h in heads]
                for i, (h, a) in enumerate(zip(heads, views)):
                    slope = 2.0 ** (-8.0 * (head_at(h) + 1) / H)
                    ins = stt(a, dist[:, t, 0:span], -slope * HD ** 0.5, b[:, i * span:(i + 1) * span], ALU.mult, ALU.add)
                done(ins)
                for h, a in zip(heads, views):
                    ins = dve.tensor_tensor_reduce(a, a, keep[:, t, 0:span], 1.0, NEVER, ALU.add, ALU.max, amax[:, t, h:h + 1])
                done(ins)
                m = amax[:, t, heads[0]:heads[-1] + 1]
                ts(m, m, -HD ** -0.5, None, ALU.mult).then_inc(S["att_shift"], 1)

            def divide(u):
                dve.wait_ge(S["att_exp"], u + 1)
                t, heads = (0, range(4 * u, 4 * u + 4)) if u < 2 else (1, range(2 * u - 4, 2 * u - 2))
                s = asum[:, t, heads[0]:heads[-1] + 1]
                done(dve.reciprocal(s, s))
                for h in heads:
                    a = (att0 if t == 0 else att1)[:, h, 0:(P, T)[t]]
                    ins = ts(a, a, asum[:, t, h:h + 1], None, ALU.mult)
                ins.then_inc(S["att_ready"], 1)

            def keep_heads(t):
                dve.wait_ge(S["pv_done"], 2 * t + 2)
                dve.tensor_copy(catT[HD:P, 0:4, t * P:(t + 1) * P], bank[4][HD:P, :].rearrange("p (k q) -> p k q", k=4)
                                ).then_inc(S["cat_dve"], 1)

            shift(0), shift(1), divide(0)
            dve.wait_ge(S["u_tanh"], 1)
            stt(flat(uT), flat(usq), 1.0, flat(uT), ALU.add, ALU.mult).then_inc(S["u_ready"], 1)
            dve.wait_ge(S["u_ready"], 1)
            dve.wait_ge(S["sgu_done"], 1)
            for g in range(4):
                src = bank[3 + g // 2][:, (g % 2) * T:(g % 2 + 1) * T].rearrange("p (n i) -> p n i", n=2)
                ins = stt(catT[:, 4 + g, :].rearrange("p (n i) -> p n i", n=2), src, sgug[:, g:g + 1],
                          bsb[:, g, :].unsqueeze(1).to_broadcast([P, 2, P]), ALU.mult, ALU.add)
            done(ins)
            stt(catT[:, 4:8, :], catT[:, 4:8, :], 0.5, uT, ALU.mult, ALU.mult).then_inc(S["bT_ready"], 1)
            shift(2), divide(1), shift(3), divide(2), shift(4), keep_heads(0), divide(3), shift(5), divide(4), divide(5)
            keep_heads(1)
            wo = [chunk_no["out", half] + 1 for half in range(2)]
            residual(0, [(0, 0, 3, S["mix_done"], 1), (1, 0, 4, S["chunk_done"], wo[0]),
                         (0, 1, 6, S["mix_done"], 2), (1, 1, 7, S["chunk_done"], wo[1])], hflat)

            def first_max(oh, src, mx, eq, n):
                done(dve.tensor_reduce(mx, src, AX, ALU.max))
                wide = mx.unsqueeze(2).to_broadcast([P, TT, n])
                done(tt(eq, src, wide, ALU.is_equal))
                done(tt(eq, eq, rank[:, 8 - n:8].unsqueeze(1).to_broadcast([P, TT, n]), ALU.mult))
                done(dve.tensor_reduce(rt_m, eq, AX, ALU.max))
                done(tt(oh, eq, rt_m.unsqueeze(2).to_broadcast([P, TT, n]), ALU.is_equal))

            def route(l):
                normed(2 * l + 1)
                scale_shift(2 * l + 1, l, 2)
                modulated(2 * l + 1, l, 2, hT)
                dve.wait_ge(S["lg_done"], l + 1)
                dve.wait_ge(S["late_in"], 16 * LATE)
                lg = v3(0, RCOLS)
                for t in range(TT):
                    ins = tt(lg[:, t, :], bank[6][:, t * 64:t * 64 + RCOLS], broute[:, l, :], ALU.add)
                done(ins)
                ohg, gmax, pg = v3(94, NG), rt[:, 72:74], rt[:, 92:94]
                first_max(ohg, lg[:, :, 0:NG], gmax, v3(102, NG), NG)
                tt(v3(74, NG), lg[:, :, 0:NG], gmax.unsqueeze(2).to_broadcast([P, TT, NG]), ALU.subtract).then_inc(S["g_shift"], 1)
                el = rt[:, 112:176].rearrange("p (t g e) -> p t g e", t=TT, g=NG)
                for t in range(TT):
                    ins = tt(el[:, t], lg[:, t, NG:RCOLS].rearrange("p (g e) -> p g e", g=NG),
                             ohg[:, t, :].unsqueeze(2).to_broadcast([P, NG, EG]), ALU.mult)
                done(ins)
                eg = v3(176, EG)
                done(dve.tensor_reduce(eg, el.rearrange("p t g e -> p t e g"), AX, ALU.add))
                oh1, oh2, e2, m1, m2 = v3(194, EG), v3(244, EG), v3(226, EG), rt[:, 192:194], rt[:, 242:244]
                first_max(oh1, eg, m1, v3(210, EG), EG)
                done(stt(e2, oh1, FAR, eg, ALU.mult, ALU.add))
                first_max(oh2, e2, m2, v3(210, EG), EG)
                tt(rt_dd, m2, m1, ALU.subtract).then_inc(S["e_pair_in"], 1)
                for oh, a in ((oh1, asg1), (oh2, asg2)):
                    for t in range(TT):
                        ins = tt(a[:, t].rearrange("p (g e) -> p g e", g=NG), ohg[:, t, :].unsqueeze(2).to_broadcast([P, NG, EG]),
                                 oh[:, t, :].unsqueeze(1).to_broadcast([P, NG, EG]), ALU.mult)
                done(ins)
                tt(asg[:], asg1, asg2, ALU.add).then_inc(S["asg_ready"], 1)
                dve.wait_ge(S["e_group"], l + 1)
                done(dve.tensor_reduce(rt[:, 90:92], v3(82, NG), AX, ALU.add))
                done(dve.reciprocal(pg, rt[:, 90:92]))
                dve.wait_ge(S["e_pair"], l + 1)
                g1, g2 = rt[:, 266:268], rt[:, 268:270]
                done(ts(rt[:, 264:266], rt_q, 1.0, None, ALU.add))
                done(dve.reciprocal(rt[:, 264:266], rt[:, 264:266]))
                done(tt(g1, pg, rt[:, 264:266], ALU.mult))
                done(tt(g2, g1, rt_q, ALU.mult))
                dve.wait_ge(S["tot_done"], l + 1)
                dve.tensor_copy(tot[0:NE, :], bank[7][0:NE, 64:64 + P]).then_inc(S["tot_ready"], 1)
                dve.wait_ge(S["off_done"], l + 1)
                off, cnt, r128 = rt[:, 690:722], rt[:, 722:723], rt[:, 723:724]
                done(dve.tensor_copy(off, bank[7][:, 192:192 + NE]))
                done(dve.tensor_reduce(cnt, bank[7][:, 224:224 + NE], AX, ALU.max))
                pos = rt[:, 462:526].rearrange("p (t e) -> p t e", t=TT)
                done(tt(pos, bank[7][:, 0:2 * NE].rearrange("p (t e) -> p t e", t=TT),
                        off.unsqueeze(1).to_broadcast([P, TT, NE]), ALU.add))
                slot = []
                for n, a in enumerate((asg1, asg2)):
                    done(tt(a, a, pos, ALU.mult))
                    slot.append(rt[:, 724 + 2 * n:726 + 2 * n])
                    done(dve.tensor_reduce(slot[n], a, AX, ALU.add))
                for t in range(TT):
                    s1, s2 = slot[0][:, t:t + 1], slot[1][:, t:t + 1]
                    done(ts(pick[:, t, :], slot_no[:], s2, None, ALU.is_equal))
                    ins = stt(sel[:, t, :], slot_no[:], s1, pick[:, t, :], ALU.is_equal, ALU.add)
                ins.then_inc(S["sel_ready"], 1)
                dve.wait_ge(S["sel_ready"], l + 1)
                for t in range(TT):
                    s1, s2 = slot[0][:, t:t + 1], slot[1][:, t:t + 1]
                    ts(pick[:, t, :], slot_no[:], s2, g2[:, t:t + 1], ALU.is_equal, ALU.mult)
                    done(ts(comb[:, t, :], slot_no[:], s1, g1[:, t:t + 1], ALU.is_equal, ALU.mult))
                    ins = tt(comb[:, t, :], comb[:, t, :], pick[:, t, :], ALU.add)
                ins.then_inc(S["comb_ready"], 1)
                done(ts(r128, cnt, float(WIN), float(WIN), ALU.is_gt, ALU.mult))
                ts(win_i[0:1, 0:NE], off[0:1, :], r128[0:1, :], float(SLOTS), ALU.add, ALU.min)
                dve.tensor_copy(win_i[0:1, NE:2 * NE], off[0:1, :])
                ts(grp_i[0:1, l:l + 1], r128[0:1, :], NE / XS / WIN, None, ALU.mult).then_inc(S["win_ready"], 1)
                dve.memset(xgT[:, :, SLOTS:PADDED], 0.0)
                for k in range(1, KT, 2):
                    dve.wait_ge(S["xg_done"], KT * l + k + 1)
                    ts(xgT[:, k, 0:SLOTS], bank[2 + k % 4][:, :], ab[:, l, 2, k:k + 1], ab[:, l, 3, k:k + 1],
                       ALU.mult, ALU.add).then_inc(S["xg_dve"], 1)
                if l == 0:
                    dve.wait_ge(S["mod_kept"], 24)
                    dve.wait_ge(S["row_done"], 1)
                    for half in range(2):
                        at = slice(half * HALF, (half + 1) * HALF)
                        ins = tt(gates[:, 2, at], gates[:, 2, at], bank[2 + 2 * half][:, :], ALU.mult)
                    ins.then_inc(S["row_kept"], 1)

            def experts(l):
                e = E[l]

                def window(j, b):
                    start = dve.value_load(win_i[0:1, bass.ds(j, 1)], min_val=0, max_val=SLOTS)
                    if not isinstance(j, int) or j >= 2:
                        dve.wait_ge(e["gu_done"], j - 1)
                    dve.tensor_copy(xw[:, b % 2], xgT[:, :, bass.ds(start, WIN)]).then_inc(e["xw_ready"], 1)

                def silu_mul(j, b):
                    dve.wait_ge(e["gu_tanh"], j + 1)
                    g, u = bank[b % 2][:, 0:FE], bank[b % 2][:, FE:2 * FE]
                    if not isinstance(j, int) or j >= 2:
                        dve.wait_ge(e["act_ready"], j - 1)
                    stt(gl[:, b % 2, :], th[:, b % 2, :], 1.0, g, ALU.add, ALU.mult).then_inc(e["gl_ready"], 1)
                    dve.wait_ge(e["gl_ready"], j + 1)
                    if not isinstance(j, int) or j >= 2:
                        dve.wait_ge(e["act_turned"], j - 1)
                    stt(act_s[:, b % 2].rearrange("s t p -> s p t"), gl[:, b % 2, :].rearrange("s (p t) -> s p t", t=FT), 0.5,
                        u.rearrange("s (p t) -> s p t", t=FT), ALU.mult, ALU.mult).then_inc(e["act_ready"], 1)

                def keep_y(j, b, signal):
                    start = dve.value_load(win_i[0:1, bass.ds(j, 1)], min_val=0, max_val=SLOTS)
                    dve.wait_ge(e["down_done"], j + 1)
                    if not isinstance(j, int) or j >= 1:
                        dve.wait_ge(e["y_dve"], j)
                    dve.tensor_copy(yT[:, 4:8, bass.ds(start, WIN)], bank[5 + 2 * (b % 2)][:, :].rearrange("p (k s) -> p k s", k=4)
                                    ).then_inc(signal, 1)

                def group(i):
                    for b in range(XS):
                        n = i * XS + b if isinstance(i, int) else XS
                        window(i * XS + b, b)
                        if n >= 1:
                            silu_mul(i * XS + (b - 1), (b - 1) % XS)
                        if n >= 2:
                            keep_y(i * XS + (b - 2), (b - 2) % XS, e["y_dve"])

                dve.wait_ge(S["win_ready"], l + 1)
                dve.wait_ge(S["xg_act"], 4 * (l + 1))
                dve.wait_ge(S["xg_dve"], 4 * (l + 1))
                dve.wait_ge(S["lg_done"], l + 1)
                groups = dve.value_load(grp_i[0:1, l:l + 1], min_val=0, max_val=NE // XS) + NE // XS
                group(0)
                with dve.Fori(1, groups) as i:
                    group(i)
                silu_mul(groups * XS - 1, XS - 1)
                keep_y(groups * XS - 2, XS - 2, e["y_dve"])
                keep_y(groups * XS - 1, XS - 1, e["y_last_dve"])

            def combine(l):
                for s in range(4):
                    dve.wait_ge(S["y_turned"], 8 * l + 2 * s + 2)
                    dve.tensor_copy(ysl[:, s, HALF:D], bank[2 * (s % 2) + 1][:, :]).then_inc(S["ysl_dve"], 1)
                n = (2, 10)[l]
                residual((1, 3)[l], [(i % 2, i // 2, 4 + i, S["mix_done"], n + i + 1) for i in range(4)], hflat)

            route(0)
            experts(0)
            combine(0)

            normed(2)
            scale_shift(2, 1, 0)
            done(dve.reciprocal(edge[:], edge[:]))
            dve.memset(hp[:, :, 0:PAD], 0.0)
            dve.memset(sA[:, :, 0:PAD], 0.0)
            done(dve.memset(sB[:, :, 0:PAD], 0.0))
            modulated(2, 1, 0, hp[:, :, PAD:PAD + T])
            dve.wait_ge(S["hT_act"], 12)
            dve.wait_ge(S["hT_dve"], 12)
            src, dst = hp, sA
            for g in range(4):
                step, win = 2 ** g, 2 ** (g + 1)
                done(tt(dst[:, 2 * g:KT, PAD:PAD + T], src[:, 2 * g:KT, PAD:PAD + T],
                        src[:, 2 * g:KT, PAD - step:PAD + T - step], ALU.add))
                y, h = dst[:, 2 * g:2 * g + 2, PAD:PAD + T], hp[:, 2 * g:2 * g + 2, PAD:PAD + T]
                done(stt(hT[:, 2 * g:2 * g + 2, win - 1:T], y[:, :, win - 1:T], 1.0 / win, h[:, :, win - 1:T], ALU.mult, ALU.subtract))
                for i in range(2):
                    done(tt(y[:, i, 0:win - 1], y[:, i, 0:win - 1], edge[:, 0:win - 1], ALU.mult))
                tt(hT[:, 2 * g:2 * g + 2, 0:win - 1], y[:, :, 0:win - 1], h[:, :, 0:win - 1], ALU.subtract
                   ).then_inc(S["pool_ready"], 1)
                src, dst = dst, (sB if g % 2 == 0 else sA)
            residual(2, [(i % 2, i // 2, 4 + i, S["mix_done"], 6 + i + 1) for i in range(4)], ar(6528, 1024))

            route(1)
            experts(1)
            combine(1)
            normed(4, write=False)
            dve.wait_ge(S["row_done"], 2)
            for t in range(TT):
                for half in range(2):
                    at = slice(half * HALF, (half + 1) * HALF)
                    ins = stt(xn[:, t, at], x_res[:, t, at], stat[:, 4 + t:5 + t], bank[2 + half][:, :], ALU.mult, ALU.mult)
                ins.then_inc(S["out_ready"], 1)


INPUTS = ["x", "c", "w_mod", "b_mod", "norm_mix", "norm_ffn", "w_in", "kv_norm", "w_kv_up", "sgu_norm", "w_s", "b_s", "w_o",
          "w_pool", "pool_scale", "w_gr", "b_gr", "w_er", "b_er", "w_gate", "w_up", "w_down", "norm_out"]


def kernel(**inputs):
    import numpy as np
    import concourse.bacc as bacc
    from concourse.bass_utils import run_bass_kernel_spmd

    nc = bacc.Bacc("TRN2", target_bir_lowering=False, num_devices=1)
    arrays, args = {}, []
    for name in INPUTS:
        a = np.ascontiguousarray(inputs[name])
        arrays[f"in_{name}"] = a
        args.append(nc.dram_tensor(f"in_{name}", a.shape, mybir.dt.from_np(a.dtype), kind="ExternalInput").ap())
    out = nc.dram_tensor("out_0", inputs["x"].shape, F32, kind="ExternalOutput").ap()
    trunk(nc, *args, out)
    r = run_bass_kernel_spmd(nc, [arrays], core_ids=[0])
    return r.results[0]["out_0"]
```

```python
from contextlib import ExitStack

import concourse.bass as bass
from concourse import mybir

F32 = mybir.dt.float32
F32R = mybir.dt.float32r
I32 = mybir.dt.int32
ALU = mybir.AluOpType
ACT = mybir.ActivationFunctionType
AX = mybir.AxisListType.X

P = 128
EPS = 1e-6
CHUNK = 64
GELU_A, GELU_C = 0.044715, 0.7978845608028654
NEVER = -(2.0 ** 126)
TAKEN = -(2.0 ** 127)
FAR = -(2.0 ** 100)


def trunk(nc, x, c, w_mod, b_mod, norm_mix, norm_ffn, w_in, kv_norm, w_kv_up, sgu_norm, w_s, b_s, w_o,
          w_pool, pool_scale, w_gr, b_gr, w_er, b_er, w_gate, w_up, w_down, norm_out, out):
    T, D = x.shape[1:]
    L, NE, _, FE = w_gate.shape
    NG = w_gr.shape[2]
    EG = NE // NG
    TT, KT, FT = T // P, D // P, FE // P
    H, HD = 8, 64
    LAT = kv_norm.shape[1]
    HALF = 512
    SLOTS = 2 * T
    WIN = 64
    PASSES = T // WIN
    PADDED = SLOTS + WIN
    TOPK = min(256, T // 4)
    BW = w_s.shape[1] * P
    Q0, KV0, QI0, KI0, U0, V0 = 0, 512, 640, 1152, 1224, 1736
    RCOLS = NG + NE
    assert (T, D, L, NE, FE, NG, LAT, BW) == (256, 1024, 2, 32, 256, 4, 128, 512)

    with ExitStack() as ctx:
        def sb(name, shape, dt=F32):
            return ctx.enter_context(nc.sbuf_tensor(name, shape, dt))

        def sem(name):
            return ctx.enter_context(nc.semaphore(name))

        CH = 4
        XS = 4
        ring = sb("ring", [P, CH * KT * HALF])
        dn_w = sb("dn_w", [P, 2, FT, D])
        UT = 2
        UN = KT // UT
        parts = sb("parts", [P, 2, 2, UT, HALF], F32R)
        xw = sb("xw", [P, 2, KT, 2, WIN], F32R)
        x_res = sb("x_res", [P, TT, D])
        xn = sb("xn", [P, TT, D])
        hT = sb("hT", [P, KT, T])
        gates = sb("gates", [P, 4, D])
        arena = sb("arena", [P, 11520])
        ident = sb("ident", [P, P])
        ones = sb("ones", [P, P])
        before = sb("before", [P, P])
        slot_no = sb("slot_no", [P, SLOTS])
        rows = sb("rows", [9, D])
        row_sel = sb("row_sel", [9, 6, P])
        wroute = sb("wroute", [P, L, KT, RCOLS])
        broute = sb("broute", [P, L, RCOLS])
        bias_col = sb("bias_col", [P, L, 6, KT])
        gain_col = sb("gain_col", [P, 4, KT])
        kvg = sb("kvg", [P, 1])
        sgug = sb("sgug", [P, 4])
        raw_col = sb("raw_col", [P, 8, KT])
        ab = sb("ab", [P, L, 4, KT])
        cs = sb("cs", [P, 3, KT])
        stat = sb("stat", [P, 32])
        mhalf = sb("mhalf", [P, 2])
        w8 = sb("w8", [P, TT, H])
        best = sb("best", [P, 8])
        amax = sb("amax", [P, TT, H])
        asum = sb("asum", [P, TT, H])
        edge = sb("edge", [P, 16])
        rank = sb("rank", [P, 8])
        rt = sb("rt", [P, 728])
        win_i = sb("win_i", [1, PASSES * NE], I32)
        eid_i = sb("eid_i", [1, PASSES * NE], I32)
        grp_i = sb("grp_i", [1, L], I32)

        def chunk_at(n):
            s = (n % CH) * KT * HALF
            return ring[:, s:s + KT * HALF].rearrange("p (k n) -> p k n", k=KT)

        def gu_at(s):
            return ring[:, s * KT * HALF:(s + 1) * KT * HALF].rearrange("p (w k f) -> p w k f", w=2, k=KT)

        def ar(a, n, **kw):
            v = arena[:, a:a + n]
            if kw:
                names = " ".join(kw)
                v = v.rearrange(f"p ({names} z) -> p {names} z", **kw)
            return v

        qiT, gtmp, qT, uT = ar(0, 1024, t=4), ar(1024, 1024, t=2), ar(2048, 1024, t=4), ar(3072, 1024, t=4)
        pT0, pT1 = ar(0, 1024), ar(0, 2048, s=2)
        vtk = ar(4096, 1024, t=2)
        att0 = ar(5120, 1024, h=8)
        kvn, kvnT, kidup = ar(5120, 256, t=2), ar(5376, 256), ar(5632, 256, t=2)
        relu = ar(6144, 1024, b=2)
        wkv = ar(3584, 384, w=3)
        ws_raw, usq = ar(3072, 512, g=4), ar(0, 1024, t=4)
        csb = ar(7168, 1024, k=8)
        score, keep, dist = ar(8192, 512, t=2), ar(8704, 512, t=2), ar(9216, 512, t=2)
        bsb, wsT = ar(9728, 512, g=4), ar(10240, 512, g=4)
        kiT, kT, v2 = ar(10752, 256), ar(11008, 256), ar(11264, 256, t=2)
        att1 = hT[:, :, :].rearrange("p k t -> p (k t)").rearrange("p (h s) -> p h s", h=8)
        xnf = xn[:, :, :].rearrange("p a b -> p (a b)")
        catT = xnf.rearrange("p (k t) -> p k t", k=8)
        xgT, yT, combT = ar(0, KT * PADDED, k=8), ar(4608, KT * PADDED, k=8), ar(10496, 1024, s=4)
        xn_parts = parts[:].rearrange("p b h k n -> p (b h k n)").rearrange("p (h t d) -> p h t d", h=2, t=TT)
        sel = xw[:].rearrange("p b k h s -> p (b k h s)")[:, 0:TT * SLOTS].rearrange("p (t s) -> p t s", t=TT)
        comb, comb2, pick = ar(9216, 1024, t=2), ar(10496, 1024, t=2), ar(8192, 1024, t=2)
        slot1, slot2, gate1, gate2 = rt[:, 724:726], rt[:, 726:728], rt[:, 266:268], rt[:, 268:270]
        ysl = ar(0, 4096, s=4)
        part2 = xnf[0:WIN, 0:1024].rearrange("p (b n) -> p b n", b=2)
        gu = xnf[0:WIN, 1024:2048].rearrange("p (b n) -> p b n", b=2)
        hflat = hT[:, :, :].rearrange("p k t -> p (k t)")
        th = hflat[0:WIN, 0:512].rearrange("p (b f) -> p b f", b=2)
        gl = hflat[0:WIN, 512:1024].rearrange("p (b f) -> p b f", b=2)
        act_s = hflat[:, 1024:1536].rearrange("p (b t f) -> p b t f", b=2, t=FT)
        actT = hflat[:, 1536:1792].rearrange("p (b t s) -> p b t s", b=2, t=FT)
        PAD = 16
        hp, sA, sB = ar(0, 2176, k=8), ar(2176, 2176, k=8), ar(4352, 2176, k=8)
        wpool = dn_w[:, 0].rearrange("p t d -> p (t d)").rearrange("p (g t n) -> p g t n", g=4, t=2)

        def v3(a, n):
            return rt[:, a:a + TT * n].rearrange("p (t n) -> p t n", t=TT)

        rt_gd, rt_ge, rt_dd, rt_q, rt_m = rt[:, 74:82], rt[:, 82:90], rt[:, 260:262], rt[:, 262:264], rt[:, 110:112]
        asg1, asg2, asg, tot = v3(270, NE), v3(334, NE), v3(398, NE), rt[:, 526:526 + P]

        bank = [ctx.enter_context(nc.psum_tensor(f"bank{i}", [P, 512], F32)) for i in range(8)]

        mods = [(l, v) for l in range(L) for v in range(6)]
        plan = [("mod", m) for m in range(4)] + [("in", "qi"), ("in", "kv"), ("mod", 4), ("mod", 5), ("in", "q"), ("in", "v"),
                ("mod", 6), ("mod", 7), ("in", "u"), ("mod", 8), ("mod", 9), ("out", 0), ("out", 1)]
        plan += [("mod", m) for m in (10, 11, 22, 23, *range(12, 22))]
        turn_of = {m: i for i, m in enumerate(m for kind, m in plan if kind == "mod")}
        FIRST = plan.index(("mod", 12))
        chunk_no = {key: n for n, key in enumerate(plan)}
        chunk_dmas = [2 if key == ("in", "kv") else 1 for key in plan]

        def arrivals(n):
            return 16 * sum(chunk_dmas[i] for i in range(n % CH, n + 1, CH))

        GATE = {(0, 2): 0, (0, 5): 1, (1, 2): 2, (1, 5): 3}
        def on_pe(m):
            return 3 if m < 4 or 12 <= m < 16 or m in (20, 21) else 0

        def row_at(m):
            return gates[0:1, 3, :] if m < 12 else rows[0:1, :]

        BY_POOL = [10, 11, 22, 23, 16, 17, 18, 19]
        by_dve = [m for m in range(24) if m not in BY_POOL]

        columns = [v for v in mods if v not in GATE]
        ROW_BIAS = {(0, 2): 0, (0, 5): 1, (1, 2): 2, (1, 5): 3, (1, 0): 7, (1, 1): 8}

        names = """c_in x_in early_in small_in late_in consts c_tanh csb_ready
            chunk_done acc_dve scaled acc_pool xn_part1 xn_part2 wpool_in mod_kept col_done col_kept ab_ready
            square_sum mean_sq inv_rms xn_ready xT_done hT_act hT_dve x_ready
            ws_turned wsT_copied wsT_ready gain_row gain_ready
            qi_done qi_kept kv_sq kv_ms kv_inv wkv_ready kv_ready kt_turned kiT_ready kvnT_ready
            kup_done kup_kept q_done q_kept v_done v_kept v_poly v_tanh ln_ms ln_inv vln_ready
            u_done u_kept u_poly u_tanh u_ready score_done score_relu score_added
            att_done att_shift att_exp att_ready p_turned pT_ready pv_done cat_act cat_dve
            mix_done sgu_done bT_ready
            lg_done g_shift e_group e_pair_in e_pair asg_ready tot_done tot_ready off_done
            sel_ready comb_ready xg_done xg_act xg_dve win_ready comb_turned combT_ready
            row_done pool_ready y_turned ysl_act ysl_dve out_ready out_stored dve_own pool_own""".split()
        S = {n: sem(n) for n in names}
        chunk_in = [sem(f"chunk_in{i}") for i in range(CH)]
        gu_in = [[sem(f"gu_in{l}_{i}") for i in range(XS)] for l in range(L)]
        dn_in = [[sem(f"dn_in{l}_{i}") for i in range(2)] for l in range(L)]
        E = [{n: sem(f"{n}{l}") for n in ("xw_part1", "xw_ready", "part1_ready", "parts_ready", "unit_done", "part2_kept",
                                          "gu_ready", "gu_tanh", "gl_ready", "act_ready", "act_turned", "actT_ready",
                                          "down_done", "y_act", "y_dve", "y_last_act", "y_last_dve")} for l in range(L)]

        def head_at(place):
            return 2 * (place % (H // 2)) + place // (H // 2)

        def xslot(l, j):
            return ((FIRST, len(plan))[l] + j) % XS

        EARLY, SMALL, LATE = 4, 14, 4 * L

        block = ctx.enter_context(nc.Block())

        @block.sync
        def _(sp):
            sp.dma_start(cs[:, 0, :], c.rearrange("b (p k) -> p (b k)", p=P)).then_inc(S["c_in"], 16)
            for t in range(TT):
                sp.dma_start(x_res[:, t, :], x[0, t * P:(t + 1) * P, :]).then_inc(S["x_in"], 16)
            win_in = w_in[0].rearrange("(p k) n -> p k n", k=KT)

            def chunk(n):
                kind, what = plan[n]
                dst, arrived = chunk_at(n), chunk_in[n % CH]
                if kind == "mod":
                    l, v = mods[what // 2]
                    a = v * D + (what % 2) * HALF
                    sp.dma_start(dst, w_mod[l].rearrange("(p k) n -> p k n", k=KT)[:, :, a:a + HALF]).then_inc(arrived, 16)
                elif kind == "out":
                    sp.dma_start(dst, w_o[0].rearrange("(k p) n -> p k n", p=P)[:, :, what * HALF:(what + 1) * HALF]
                                 ).then_inc(arrived, 16)
                elif what == "kv":
                    sp.dma_start(dst[:, :, 0:LAT], win_in[:, :, KV0:KV0 + LAT]).then_inc(arrived, 16)
                    sp.dma_start(dst[:, :, LAT:LAT + 72], win_in[:, :, KI0:KI0 + 72]).then_inc(arrived, 16)
                else:
                    a = {"qi": QI0, "q": Q0, "v": V0, "u": U0}[what]
                    sp.dma_start(dst, win_in[:, :, a:a + HALF]).then_inc(arrived, 16)

            for n in range(FIRST):
                if n >= CH:
                    sp.wait_ge(S["chunk_done"], n - CH + 1)
                chunk(n)

            def gate_up(l, s, e):
                for w, src in enumerate((w_gate, w_up)):
                    sp.dma_start(gu_at(s)[:, w], src[l][bass.ds(e, 1)].rearrange("o (p k) f -> p (o k) f", k=KT)
                                 ).then_inc(gu_in[l][s], 16)

            def down(l, b, e):
                sp.dma_start(dn_w[:, b], w_down[l][bass.ds(e, 1)].rearrange("o (p t) d -> p (o t) d", t=FT)
                             ).then_inc(dn_in[l][b], 16)

            def expert_at(j):
                return sp.value_load(eid_i[0:1, bass.ds(j, 1)], min_val=0, max_val=NE - 1)

            for l in range(L):
                for j in range(XS):
                    sp.wait_ge(S["chunk_done"], (FIRST, len(plan))[l] - CH + 1 + j)
                    gate_up(l, xslot(l, j), j)
                    if l == 1 and j == 2:
                        sp.wait_ge(S["mix_done"], 10)
                    if j >= 2:
                        down(l, j % 2, j - 2)
                sp.wait_ge(S["win_ready"], l + 1)
                groups = sp.value_load(grp_i[0:1, l:l + 1], min_val=0, max_val=(PASSES - 1) * NE // XS) + NE // XS
                with sp.Fori(1, groups) as i:
                    for b in range(XS):
                        e = expert_at(i * XS + b)
                        sp.wait_ge(E[l]["parts_ready"], i * (XS * UN) + UN * (b + 1 - XS))
                        gate_up(l, xslot(l, b), e)
                        e = expert_at(i * XS + (b - 2))
                        sp.wait_ge(E[l]["down_done"], i * XS + (b - 3))
                        down(l, b % 2, e)
                sp.wait_ge(E[l]["down_done"], groups * XS - 3)
                down(l, 0, NE - 2)
                sp.wait_ge(E[l]["down_done"], groups * XS - 2)
                down(l, 1, NE - 1)
                if l == 0:
                    for n in range(FIRST, len(plan)):
                        if n < FIRST + XS:
                            sp.wait_ge(E[l]["parts_ready"], groups * (XS * UN) + UN * (n - FIRST + 1 - XS))
                        else:
                            sp.wait_ge(S["chunk_done"], n - CH + 1)
                        chunk(n)
                        if n == FIRST + 1:
                            sp.wait_ge(E[l]["down_done"], groups * XS - 1)
                            sp.dma_start(wpool, w_pool[0].rearrange("g (t p) n -> p g t n", p=P)).then_inc(S["wpool_in"], 16)
            sp.wait_ge(S["out_ready"], TT)
            for t in range(TT):
                sp.dma_start(out[0, t * P:(t + 1) * P, :], xn[:, t, :]).then_inc(S["out_stored"], 16)
            sp.wait_ge(S["out_stored"], 16 * TT)

        @block.gpsimd
        def _(pool):
            own = 0

            def done(ins):
                nonlocal own
                own += 1
                ins.then_inc(S["pool_own"], 1)
                pool.wait_ge(S["pool_own"], own)

            done(pool.memset(ident[:], 0.0))
            done(pool.affine_select(out=ident[:], in_=ident[:], compare_op=ALU.not_equal, fill=1.0, base=0,
                                    pattern=[[-1, P]], channel_multiplier=1))
            done(pool.memset(mhalf[:], -0.5))
            done(pool.memset(ones[:], 1.0))
            pool.sem_inc(S["consts"], 1)

            def power(n):
                pool.wait_ge(S["mean_sq"], n + 1)
                pool.tensor_tensor(stat[:, 4:6], stat[:, 2:4], mhalf[:], ALU.pow).then_inc(S["inv_rms"], 1)

            for n, (dst, src) in enumerate(((bias_col[:, 0], b_mod[0].rearrange("(v p k) -> p v k", v=6, k=KT)),
                             (gain_col[:, 0], norm_mix[0].rearrange("(p k) -> p k", k=KT)),
                             (kvg[:], kv_norm[0].rearrange("(p o) -> p o", o=1)),
                             (wkv[:, 0, :], w_kv_up[0]),
                             (rows[0:1], b_mod[0:1, 2 * D:3 * D]), (rows[1:2], b_mod[0:1, 5 * D:6 * D]),
                             (rows[2:3], b_mod[1:2, 2 * D:3 * D]), (rows[3:4], b_mod[1:2, 5 * D:6 * D]),
                             (rows[4:5], pool_scale[0:1]), (rows[5:6], norm_out.rearrange("(o d) -> o d", o=1)),
                             (rows[6:7], norm_mix[1:2]), (rows[7:9], b_mod[1, 0:2 * D].rearrange("(v d) -> v d", v=2)),
                             (ws_raw, w_s[0].rearrange("g i j -> i g j")),
                             (bias_col[:, 1], b_mod[1].rearrange("(v p k) -> p v k", v=6, k=KT)),
                             (gain_col[:, 1], norm_ffn[0].rearrange("(p k) -> p k", k=KT)),
                             (gain_col[:, 2], norm_ffn[1].rearrange("(p k) -> p k", k=KT)),
                             (sgug[:], sgu_norm[0].rearrange("(g p) -> p g", p=P)),
                             (bsb, b_s[0].partition_broadcast(P)))):
                pool.dma_start(dst, src, allow_slow_non_contiguous=True).then_inc(S["early_in" if n < EARLY else "small_in"], 16)
                if n == EARLY - 1:
                    power(0)
            for l in range(L):
                for dst, src in ((wroute[:, l, :, 0:NG], w_gr[l].rearrange("(p k) n -> p k n", k=KT)),
                                 (wroute[:, l, :, NG:RCOLS], w_er[l].rearrange("(p k) n -> p k n", k=KT)),
                                 (broute[:, l, 0:NG], b_gr[l].partition_broadcast(P)),
                                 (broute[:, l, NG:RCOLS], b_er[l].partition_broadcast(P))):
                    pool.dma_start(dst, src).then_inc(S["late_in"], 16)
            done(pool.memset(row_sel[:], 0.0))
            done(pool.affine_select(out=row_sel[:], in_=row_sel[:], compare_op=ALU.not_equal, fill=1.0, base=0,
                                    pattern=[[-1, 6], [0, P]], channel_multiplier=1))
            done(pool.memset(before[:], 1.0))
            done(pool.affine_select(out=before[:], in_=before[:], compare_op=ALU.is_gt, fill=0.0, base=0,
                                    pattern=[[1, P]], channel_multiplier=-1))
            done(pool.iota(slot_no[:], [[1, SLOTS]], base=0, channel_multiplier=0, allow_small_or_imprecise_dtypes=True))
            for t in range(TT):
                done(pool.iota(dist[:, t, :], [[-1, T]], base=t * P, channel_multiplier=1,
                               allow_small_or_imprecise_dtypes=True))
            done(pool.iota(edge[:], [[1, 16]], base=1, channel_multiplier=0, allow_small_or_imprecise_dtypes=True))
            done(pool.iota(rank[:], [[-1, 8]], base=8, channel_multiplier=0, allow_small_or_imprecise_dtypes=True))
            done(pool.iota(eid_i[:], [[0, PASSES], [1, NE]], base=0, channel_multiplier=0))
            pool.sem_inc(S["consts"], 1)

            pool.wait_ge(S["kv_ms"], 1)
            pool.tensor_tensor(stat[:, 10:12], stat[:, 8:10], mhalf[:], ALU.pow).then_inc(S["kv_inv"], 1)
            pool.wait_ge(S["ln_ms"], 1)
            pool.tensor_tensor(stat[:, 18:20], stat[:, 16:18], mhalf[:], ALU.pow).then_inc(S["ln_inv"], 1)
            def add_up(ms):
                for m in ms:
                    w = chunk_at(chunk_no["mod", m])
                    pool.wait_ge(S["scaled"], BY_POOL.index(m) + 1)
                    done(pool.tensor_tensor(w[:, 0:4, :], w[:, 0:4, :], w[:, 4:8, :], ALU.add))
                    done(pool.tensor_tensor(w[:, 0:2, :], w[:, 0:2, :], w[:, 2:4, :], ALU.add))
                    pool.tensor_tensor(w[:, 0, :], w[:, 0, :], w[:, 1, :], ALU.add).then_inc(S["acc_pool"], 1)

            def split_tokens(l):
                pool.wait_ge(S["xn_part1"], l + 1)
                for t in range(TT):
                    ins = pool.tensor_tensor(xn_parts[:, 1, t], xn[:, t, :], xn_parts[:, 0, t].bitcast(F32), ALU.subtract)
                ins.then_inc(S["xn_part2"], 1)

            def gates_by_slot(l):
                pool.wait_ge(S["sel_ready"], l + 1)
                for t in range(TT):
                    pool.tensor_scalar(comb2[:, t, :], slot_no[:], slot2[:, t:t + 1], gate2[:, t:t + 1], ALU.is_equal, ALU.mult)
                    done(pool.tensor_scalar(comb[:, t, :], slot_no[:], slot1[:, t:t + 1], gate1[:, t:t + 1], ALU.is_equal, ALU.mult))
                    ins = pool.tensor_tensor(comb[:, t, :], comb[:, t, :], comb2[:, t, :], ALU.add)
                ins.then_inc(S["comb_ready"], 1)

            add_up((10, 11))
            power(1)
            split_tokens(0)
            add_up((22, 23))
            gates_by_slot(0)
            add_up((16, 17))
            power(2)
            add_up((18, 19))
            power(3)
            split_tokens(1)
            gates_by_slot(1)
            power(4)

        @block.tensor
        def _(pe):
            def arrived(key):
                n = chunk_no[key]
                pe.wait_ge(chunk_in[n % CH], arrivals(n))
                return chunk_at(n)

            def turned(src, t, k, natural):
                return src[:, t, k * P:(k + 1) * P] if natural else src[:, t, :].rearrange("p (q k) -> p k q", k=KT)[:, k]

            def mod_chunk(m):
                vec, half = mods[m // 2], m % 2
                w = arrived(("mod", m))
                i = turn_of[m]
                if i >= 2:
                    pe.wait_ge(S["mod_kept"], i - 1)
                    before_it = next(mods[x // 2] for x in turn_of if turn_of[x] == i - 2)
                    if m % 2 and before_it in columns:
                        pe.wait_ge(S["col_kept"], columns.index(before_it) + 1)
                if m == 11:
                    pe.wait_ge(S["pT_ready"], 6)
                wide = vec in GATE
                o = bank[m % 2][:, :] if wide else bank[m % 2][0:1, :]
                if vec in ROW_BIAS:
                    r = ROW_BIAS[vec]
                    pe.matmul(o, row_sel[:, r, :] if wide else ident[0:9, r:r + 1],
                              rows[:, half * HALF:(half + 1) * HALF], start=True, stop=False)
                for k in range(on_pe(m)):
                    pe.matmul(o, csb[:, k, :] if wide else cs[:, 2, k:k + 1], w[:, k, :],
                              start=(k == 0 and vec not in ROW_BIAS), stop=False)
                if m in BY_POOL:
                    pe.wait_ge(S["acc_pool"], BY_POOL.index(m) + 1)
                else:
                    pe.wait_ge(S["acc_dve"], by_dve.index(m) + 1)
                ins = pe.matmul(o, ones[:] if wide else ones[:, 0:1], w[:, 0 if m in BY_POOL else KT - 1, :],
                                start=(on_pe(m) == 0 and vec not in ROW_BIAS), stop=True)
                ins.then_inc(S["chunk_done"], 1)

            def column(v):
                vec = columns[v]
                pe.wait_ge(S["mod_kept"], turn_of[2 * mods.index(vec) + 1] + 1)
                for k in range(KT):
                    src = turned(row_at(2 * mods.index(vec)).unsqueeze(1), 0, k, natural=vec in ((1, 0), (1, 1)))
                    ins = pe.matmul(bank[1][:, k:k + 1], src, ones[0:1, 0:1], start=True, stop=True)
                ins.then_inc(S["col_done"], 1)

            def mod_run(ms):
                waiting = None
                for m in ms:
                    mod_chunk(m)
                    if waiting is not None:
                        column(waiting)
                        waiting = None
                    if m % 2 and mods[m // 2] in columns:
                        waiting = columns.index(mods[m // 2])
                if waiting is not None:
                    column(waiting)

            def turn(n, natural=False):
                pe.wait_ge(S["xn_ready"], n + 1)
                for kk in range(4):
                    for k in (2 * kk, 2 * kk + 1):
                        for t in range(TT):
                            a = (k % 2) * T + t * P
                            ins = pe.transpose(bank[2 + kk][:, a:a + P], turned(xn, t, k, natural), ident[:])
                    ins.then_inc(S["xT_done"], 1)

            def hT_ready(n):
                pe.wait_ge(S["hT_act"], 4 * n)
                pe.wait_ge(S["hT_dve"], 4 * n)

            def by_channel(key, banks, first_done):
                w = arrived(key)
                for m in range(4):
                    for k in range(KT):
                        ins = pe.matmul(bank[banks[m // 2]][:, (m % 2) * T:(m % 2 + 1) * T], w[:, k, m * P:(m + 1) * P],
                                        hT[:, k, :], start=(k == 0), stop=(k == KT - 1))
                    if m == 1:
                        ins.then_inc(first_done, 1)
                ins.then_inc(S["chunk_done"], 1)

            pe.wait_ge(S["consts"], 1)
            turn(0)
            pe.wait_ge(S["csb_ready"], 1)
            mod_run(range(0, 4))
            hT_ready(1)
            by_channel(("in", "qi"), (6, 7), S["qi_done"])
            w = arrived(("in", "kv"))
            for t in range(TT):
                for k in range(KT):
                    ins = pe.matmul(bank[2][:, t * 200:(t + 1) * 200], hT[:, k, t * P:(t + 1) * P], w[:, k, 0:200],
                                    start=(k == 0), stop=(k == KT - 1))
            ins.then_inc(S["chunk_done"], 1)
            pe.wait_ge(S["small_in"], 16 * SMALL)
            pe.wait_ge(S["consts"], 2)
            mod_run(range(4, 6))
            pe.wait_ge(S["kv_ready"], 1)
            for t in range(TT):
                pe.transpose(bank[5][:, t * P:(t + 1) * P], kidup[:, t, :], ident[:])
            for t in range(TT):
                ins = pe.transpose(bank[5][:, T + t * P:T + (t + 1) * P], kvn[:, t, :], ident[:])
            ins.then_inc(S["kt_turned"], 1)

            def head_units(lhs, rhs, banks, done, consumed):
                for u in range(6):
                    t, per = (0, 4) if u < 2 else (1, 2)
                    h0, span = (4 * u, P) if t == 0 else (2 * (u - 2), T)
                    if u >= 3:
                        pe.wait_ge(consumed, u - 2)
                    for i in range(per):
                        r, k = divmod(h0 + i, 4)
                        r *= HD
                        ins = pe.matmul(bank[banks[u % 3]][:, i * span:(i + 1) * span],
                                        lhs[r:r + HD, k, t * P:(t + 1) * P], rhs[r:r + HD, 0:span],
                                        start=True, stop=True)
                    ins.then_inc(done, 1)

            pe.wait_ge(S["kiT_ready"], 1)
            pe.wait_ge(S["qi_kept"], 2)
            head_units(qiT, kiT, (3, 4, 6), S["score_done"], S["score_relu"])
            for g in range(4):
                ins = pe.transpose(bank[7][:, g * P:(g + 1) * P], ws_raw[:, g, :], ident[:])
            ins.then_inc(S["ws_turned"], 1)
            for k in range(KT):
                ins = pe.matmul(bank[2][:, k:k + 1], rows[:, k * P:(k + 1) * P], ident[0:9, 6:7], start=True, stop=True)
            ins.then_inc(S["gain_row"], 1)
            pe.wait_ge(S["kvnT_ready"], 1)
            pe.wait_ge(S["wsT_copied"], 1)
            by_channel(("in", "q"), (5, 7), S["q_done"])
            pe.wait_ge(S["score_relu"], 5)
            w = arrived(("in", "v"))
            for t in range(TT):
                for k in range(KT):
                    ins = pe.matmul(bank[3 + t][:, :], hT[:, k, t * P:(t + 1) * P], w[:, k, :],
                                    start=(k == 0), stop=(k == KT - 1))
                ins.then_inc(S["v_done"] if t == 0 else S["chunk_done"], 1)
            mod_run(range(6, 8))
            pe.wait_ge(S["gain_ready"], 1)
            pe.wait_ge(S["wkv_ready"], 1)
            pe.matmul(bank[2][:, 0:T], wkv[:, 1, :], kvnT, start=True, stop=True)
            for t in range(TT):
                ins = pe.matmul(bank[2][:, T + t * P:T + (t + 1) * P], kvnT[:, t * P:(t + 1) * P], wkv[:, 2, :],
                                start=True, stop=True)
            ins.then_inc(S["kup_done"], 1)
            pe.wait_ge(S["score_relu"], 6)
            pe.wait_ge(S["q_kept"], 1)
            by_channel(("in", "u"), (6, 5), S["u_done"])
            mod_run(range(8, 10))
            pe.wait_ge(S["vln_ready"], 1)
            pe.wait_ge(S["wsT_ready"], 1)
            for t in range(TT):
                for g in range(4):
                    a = (g % 2) * T + t * P
                    ins = pe.matmul(bank[3 + g // 2][:, a:a + P], vtk[:, t, g * P:(g + 1) * P], wsT[:, g, :],
                                    start=True, stop=True)
            ins.then_inc(S["sgu_done"], 1)
            pe.wait_ge(S["q_kept"], 2)
            pe.wait_ge(S["kup_kept"], 1)
            pe.wait_ge(S["u_kept"], 2)
            head_units(qT, kT, (6, 7, 2), S["att_done"], S["att_shift"])

            def turn_p(v):
                pe.wait_ge(S["att_ready"], v + 1)
                if v >= 2:
                    pe.wait_ge(S["pT_ready"], v - 1)
                b = bank[(5, 1)[v % 2]]
                for i in range(4):
                    src = att0[:, 4 * v + i, :] if v < 2 else att1[:, 2 * (v - 2) + i % 2, (i // 2) * P:(i // 2 + 1) * P]
                    ins = pe.transpose(b[:, i * P:(i + 1) * P], src, ident[:])
                ins.then_inc(S["p_turned"], 1)

            def values(t):
                for b in range(2):
                    for s in range(t + 1):
                        rhs = pT0[:, b * 512:(b + 1) * 512] if t == 0 else pT1[:, s, b * 512:(b + 1) * 512]
                        ins = pe.matmul(bank[3 + b][:, :], v2[:, s, :], rhs, start=(s == 0), stop=(s == t))
                    ins.then_inc(S["pv_done"], 1)

            pe.wait_ge(S["mod_kept"], 10)
            pe.wait_ge(S["col_kept"], 4)
            turn_p(0)
            turn_p(1)
            pe.wait_ge(S["pT_ready"], 2)
            pe.wait_ge(S["bT_ready"], 1)
            values(0)
            for v in range(2, 6):
                turn_p(v)
            pe.wait_ge(S["pT_ready"], 6)
            pe.wait_ge(S["cat_act"], 1)
            pe.wait_ge(S["cat_dve"], 1)
            values(1)
            pe.wait_ge(S["cat_act"], 2)
            pe.wait_ge(S["cat_dve"], 2)
            pe.wait_ge(S["att_shift"], 6)
            for half in range(2):
                w = arrived(("out", half))
                for t in range(TT):
                    for k in range(KT):
                        ins = pe.matmul(bank[(3, 4, 6, 7)[2 * half + t]][:, :], catT[:, k, t * P:(t + 1) * P], w[:, k, :],
                                        start=(k == 0), stop=(k == KT - 1))
                    ins.then_inc(S["mix_done"] if t == 0 else S["chunk_done"], 1)

            def route(l):
                mod_run((range(10, 12), range(18, 21))[l])
                turn(2 * l + 1)
                if l == 1:
                    mod_run(range(21, 22))
                hT_ready(2 * l + 2)
                pe.wait_ge(S["late_in"], 16 * LATE)
                for t in range(TT):
                    for k in range(KT):
                        ins = pe.matmul(bank[6][:, t * 64:t * 64 + RCOLS], hT[:, k, t * P:(t + 1) * P], wroute[:, l, k, :],
                                        start=(k == 0), stop=(k == KT - 1))
                ins.then_inc(S["lg_done"], 1)
                pe.wait_ge(S["asg_ready"], l + 1)
                b, a0, a1 = bank[7], asg[:, 0, :], asg[:, 1, :]
                pe.matmul(b[:, 0:NE], before[:], a0, start=True, stop=True)
                pe.matmul(b[:, NE:2 * NE], ones[:], a0, start=True, stop=False)
                pe.matmul(b[:, NE:2 * NE], before[:], a1, start=False, stop=True)
                pe.matmul(b[:, 224:224 + NE], ones[:], a0, start=True, stop=False)
                pe.matmul(b[:, 224:224 + NE], ones[:], a1, start=False, stop=True)
                pe.matmul(b[0:NE, 64:64 + P], a0, ones[:], start=True, stop=False)
                pe.matmul(b[0:NE, 64:64 + P], a1, ones[:], start=False, stop=True).then_inc(S["tot_done"], 1)
                pe.wait_ge(S["tot_ready"], l + 1)
                pe.matmul(b[:, 192:192 + NE], tot[0:NE, :], before[0:NE, 0:NE], start=True, stop=True).then_inc(S["off_done"], 1)
                pe.wait_ge(S["sel_ready"], l + 1)
                pe.wait_ge(S["xn_part2"], l + 1)
                for k in range(KT):
                    if k >= 4:
                        pe.wait_ge(S["xg_dve" if k % 2 else "xg_act"], 4 * l + (k - 4) // 2 + 1)
                    for t in range(TT):
                        for part in range(2):
                            ins = pe.matmul(bank[2 + k % 4][:, :], turned(xn_parts[:, part], t, k, False), sel[:, t, :],
                                            start=(t == 0 and part == 0), stop=(t == TT - 1 and part == 1))
                    ins.then_inc(S["xg_done"], 1)
                if l == 0:
                    mod_run(range(22, 24))

            def experts(l):
                e = E[l]

                def unit(j, b, u):
                    if u == 0:
                        pe.wait_ge(e["xw_ready"], j + 1)
                        if not isinstance(j, int) or j >= 2:
                            pe.wait_ge(e["gu_ready"], j - 1)
                    pe.wait_ge(e["parts_ready"], j * UN + (u + 1))
                    for i in range(UT):
                        k = UT * u + i
                        for part in range(2):
                            ins = pe.matmul(bank[b % 2][:, :], xw[:, b % 2, k].rearrange("p h s -> p (h s)"), parts[:, u % 2, part, i, :],
                                            start=(k == 0 and part == 0), stop=(k == KT - 1 and part == 1))
                    ins.then_inc(e["unit_done"], 1)

                def turn_act(j, b):
                    pe.wait_ge(e["act_ready"], j + 1)
                    for t in range(FT):
                        ins = pe.transpose(bank[2 + b % 2][:, t * P:(t + 1) * P], act_s[:, b % 2, t, :], ident[:])
                    ins.then_inc(e["act_turned"], 1)

                def down(j, b, loaded, quarter):
                    if quarter == 0:
                        pe.wait_ge(dn_in[l][b % 2], loaded)
                        pe.wait_ge(e["actT_ready"], j + 1)
                        if not isinstance(j, int) or j >= 2:
                            pe.wait_ge(e["y_act"], j - 1)
                            pe.wait_ge(e["y_dve"], j - 1)
                    for k in (2 * quarter, 2 * quarter + 1):
                        for t in range(FT):
                            ins = pe.matmul(bank[4 + 2 * (b % 2) + k // 4][:, (k % 4) * WIN:(k % 4 + 1) * WIN],
                                            dn_w[:, b % 2, t, k * P:(k + 1) * P], actT[:, b % 2, t, :],
                                            start=(t == 0), stop=(t == FT - 1))
                    if quarter == 3:
                        ins.then_inc(e["down_done"], 1)

                def group(i):
                    for b in range(XS):
                        j = i * XS + b
                        last = i * XS + (b - 1), (b - 1) % XS
                        loaded = i * (8 * XS) + 16 * ((b - 1) // 2 + 1)
                        first = isinstance(i, int) and j == 0
                        unit(j, b, 0)
                        unit(j, b, 1)
                        if not first:
                            turn_act(*last)
                        unit(j, b, 2)
                        if not first:
                            down(*last, loaded, 0)
                            down(*last, loaded, 1)
                        unit(j, b, 3)
                        if not first:
                            down(*last, loaded, 2)
                            down(*last, loaded, 3)

                pe.wait_ge(S["win_ready"], l + 1)
                groups = pe.value_load(grp_i[0:1, l:l + 1], min_val=0, max_val=(PASSES - 1) * NE // XS) + NE // XS
                pe.wait_ge(S["mod_kept"], (14, 24)[l])
                group(0)
                with pe.Fori(1, groups) as i:
                    group(i)
                turn_act(groups * XS - 1, XS - 1)
                for quarter in range(4):
                    down(groups * XS - 1, XS - 1, groups * (8 * XS), quarter)

            def combine(l):
                pe.wait_ge(E[l]["y_last_act"], 1)
                pe.wait_ge(E[l]["y_last_dve"], 1)
                pe.wait_ge(S["mod_kept"], (16, 24)[l])
                pe.wait_ge(S["col_kept"], 5 if l == 0 else 8)
                pe.wait_ge(S["comb_ready"], l + 1)
                for s in range(4):
                    for t in range(TT):
                        a = (s % 2) * T + t * P
                        ins = pe.transpose(bank[6 + s // 2][:, a:a + P], comb[:, t, s * P:(s + 1) * P], ident[:])
                    if s % 2:
                        ins.then_inc(S["comb_turned"], 1)
                for s in range(4):
                    for half in range(2):
                        if s >= 2:
                            pe.wait_ge(S["ysl_dve" if half else "ysl_act"], 4 * l + s - 1)
                        for k in range(4):
                            ins = pe.transpose(bank[2 * (s % 2) + half][:, k * P:(k + 1) * P],
                                               yT[:, 4 * half + k, s * P:(s + 1) * P], ident[:])
                        ins.then_inc(S["y_turned"], 1)
                pe.wait_ge(S["combT_ready"], 2 * l + 2)
                for s in range(4):
                    pe.wait_ge(S["ysl_act"], 4 * l + s + 1)
                    pe.wait_ge(S["ysl_dve"], 4 * l + s + 1)
                    for half in range(2):
                        for t in range(TT):
                            ins = pe.matmul(bank[4 + 2 * half + t][:, :], combT[:, s, t * P:(t + 1) * P],
                                            ysl[:, s, half * HALF:(half + 1) * HALF], start=(s == 0), stop=(s == 3))
                            if s == 3:
                                ins.then_inc(S["mix_done"], 1)

            route(0)
            experts(0)
            mod_run(range(12, 14))
            combine(0)
            mod_run(range(14, 16))
            turn(2, natural=True)
            mod_run(range(16, 18))
            pe.wait_ge(S["wpool_in"], 16)
            for g in range(4):
                pe.wait_ge(S["pool_ready"], g + 1)
                for t in range(TT):
                    for i in range(2):
                        ins = pe.matmul(bank[4 + 2 * (g // 2) + t][:, (g % 2) * 256:(g % 2 + 1) * 256],
                                        hT[:, 2 * g + i, t * P:(t + 1) * P], wpool[:, g, i, :], start=(i == 0), stop=(i == 1))
                    if g % 2:
                        ins.then_inc(S["mix_done"], 1)
            pe.wait_ge(S["hT_act"], 12)
            pe.wait_ge(S["hT_dve"], 12)
            for half in range(2):
                ins = pe.matmul(bank[2 + half][:, :], row_sel[:, 4, :], rows[:, half * HALF:(half + 1) * HALF],
                                start=True, stop=True)
            ins.then_inc(S["row_done"], 1)
            route(1)
            experts(1)
            combine(1)
            for half in range(2):
                ins = pe.matmul(bank[2 + half][:, :], row_sel[:, 5, :], rows[:, half * HALF:(half + 1) * HALF],
                                start=True, stop=True)
            ins.then_inc(S["row_done"], 1)

        @block.scalar
        def _(act):
            def mod_run(ms):
                for m in ms:
                    vec, half = mods[m // 2], m % 2
                    act.wait_ge(S["chunk_done"], chunk_no["mod", m] + 1)
                    at = slice(half * HALF, (half + 1) * HALF)
                    if vec in GATE:
                        act.copy(gates[:, GATE[vec], at], bank[m % 2][:, :]).then_inc(S["mod_kept"], 1)
                    else:
                        act.copy(row_at(m)[:, at], bank[m % 2][0:1, :]).then_inc(S["mod_kept"], 1)
                        if half:
                            v = columns.index(vec)
                            act.wait_ge(S["col_done"], v + 1)
                            act.copy(raw_col[:, v, :], bank[1][:, 0:KT]).then_inc(S["col_kept"], 1)

            def scale(ms):
                for m in ms:
                    n = chunk_no["mod", m]
                    act.wait_ge(chunk_in[n % CH], arrivals(n))
                    for k in range(KT):
                        w = chunk_at(n)[:, k, :]
                        ins = act.activation(w, w, ACT.Identity, scale=cs[:, 2, k:k + 1])
                    ins.then_inc(S["scaled"], 1)

            def squares(n):
                if n == 0:
                    act.wait_ge(S["x_in"], 16 * TT)
                else:
                    act.wait_ge(S["x_ready"], n)
                for t in range(TT):
                    ins = act.activation(xn[:, t, :], x_res[:, t, :], ACT.Square, accum_out=stat[:, t:t + 1])
                ins.then_inc(S["square_sum"], 1)

            def modulated(n, l, which, dst):
                act.wait_ge(S["ab_ready"], n + 1)
                for k in range(4):
                    act.wait_ge(S["xT_done"], 4 * n + k // 2 + 1)
                    act.activation(dst[:, k, :], bank[2 + k // 2][:, (k % 2) * T:(k % 2 + 1) * T], ACT.Identity,
                                   scale=ab[:, l, which, k:k + 1], bias=ab[:, l, which + 1, k:k + 1]).then_inc(S["hT_act"], 1)

            act.wait_ge(S["c_in"], 16)
            act.activation(cs[:, 1, :], cs[:, 0, :], ACT.Tanh, scale=0.5).then_inc(S["c_tanh"], 1)
            squares(0)
            mod_run(range(0, 4))
            modulated(0, 0, 0, hT)
            flat = lambda v: v.rearrange("p a b -> p (a b)")
            for i, ready in enumerate((S["qi_done"], None)):
                if ready is not None:
                    act.wait_ge(ready, 1)
                else:
                    act.wait_ge(S["chunk_done"], chunk_no["in", "qi"] + 1)
                act.copy(flat(qiT[:, 2 * i:2 * i + 2, :]), bank[6 + i][:, :]).then_inc(S["qi_kept"], 1)
            act.wait_ge(S["chunk_done"], chunk_no["in", "kv"] + 1)
            for t in range(TT):
                ins = act.activation(kvn[:, t, :], bank[2][:, t * 200:t * 200 + LAT], ACT.Square, accum_out=stat[:, 6 + t:7 + t])
            ins.then_inc(S["kv_sq"], 1)
            mod_run(range(4, 6))
            act.wait_ge(S["early_in"], 16 * EARLY)
            for w in range(2):
                for i in range(2):
                    ins = act.copy(wkv[:, 1 + w, i * HD:(i + 1) * HD], wkv[:, 0, w * HD:(w + 1) * HD])
            ins.then_inc(S["wkv_ready"], 1)
            for u in range(6):
                act.wait_ge(S["score_done"], u + 1)
                if u >= 2:
                    act.wait_ge(S["score_added"], u - 1)
                act.activation(relu[:, u % 2, :], bank[(3, 4, 6)[u % 3]][:, :], ACT.Relu, scale=HD ** -0.5
                               ).then_inc(S["score_relu"], 1)
            act.wait_ge(S["ws_turned"], 1)
            act.copy(flat(wsT), bank[7][:, :]).then_inc(S["wsT_copied"], 1)
            for i, b in enumerate((5, 7)):
                if i == 0:
                    act.wait_ge(S["q_done"], 1)
                else:
                    act.wait_ge(S["chunk_done"], chunk_no["in", "q"] + 1)
                act.copy(flat(qT[:, 2 * i:2 * i + 2, :]), bank[b][:, :]).then_inc(S["q_kept"], 1)
            for t in range(TT):
                if t == 0:
                    act.wait_ge(S["v_done"], 1)
                else:
                    act.wait_ge(S["chunk_done"], chunk_no["in", "v"] + 1)
                act.copy(vtk[:, t, :], bank[3 + t][:, :])
                act.activation(gtmp[:, t, :], bank[3 + t][:, :], ACT.Square).then_inc(S["v_kept"], 1)
            mod_run(range(6, 8))
            act.wait_ge(S["kup_done"], 1)
            act.copy(arena[:, 11008:11520], bank[2][:, :]).then_inc(S["kup_kept"], 1)
            act.wait_ge(S["v_poly"], 1)
            act.activation(flat(gtmp), flat(gtmp), ACT.Tanh, scale=GELU_C).then_inc(S["v_tanh"], 1)
            act.wait_ge(S["ws_turned"], 1)
            act.wait_ge(S["score_done"], 6)
            for i, b in enumerate((6, 5)):
                if i == 0:
                    act.wait_ge(S["u_done"], 1)
                else:
                    act.wait_ge(S["chunk_done"], chunk_no["in", "u"] + 1)
                act.copy(flat(uT[:, 2 * i:2 * i + 2, :]), bank[b][:, :])
                act.activation(flat(usq[:, 2 * i:2 * i + 2, :]), bank[b][:, :], ACT.Square).then_inc(S["u_kept"], 1)
            mod_run(range(8, 10))
            act.wait_ge(S["u_poly"], 1)
            act.activation(flat(usq), flat(usq), ACT.Tanh, scale=GELU_C).then_inc(S["u_tanh"], 1)

            def exps(u):
                act.wait_ge(S["att_shift"], u + 1)
                t, heads = (0, range(4 * u, 4 * u + 4)) if u < 2 else (1, range(2 * u - 4, 2 * u - 2))
                for h in heads:
                    a = att0[:, h, :] if t == 0 else att1[:, h, :]
                    ins = act.activation(a, a, ACT.Exp, scale=HD ** -0.5, bias=amax[:, t, h:h + 1], accum_out=asum[:, t, h:h + 1])
                ins.then_inc(S["att_exp"], 1)

            def keep_p(v):
                act.wait_ge(S["p_turned"], v + 1)
                if v == 0:
                    act.wait_ge(S["u_ready"], 1)
                if v == 2:
                    act.wait_ge(S["pv_done"], 2)
                b = bank[(5, 1)[v % 2]]
                if v < 2:
                    act.copy(pT0[:, v * 512:(v + 1) * 512], b[:, :]).then_inc(S["pT_ready"], 1)
                else:
                    a = 2 * (v - 2) * P
                    act.copy(pT1[:, :, a:a + 2 * P], b[:, :].rearrange("p (s q) -> p s q", s=2)).then_inc(S["pT_ready"], 1)

            def keep_heads(t):
                act.wait_ge(S["pv_done"], 2 * t + 1)
                act.copy(catT[0:HD, 0:4, t * P:(t + 1) * P], bank[3][0:HD, :].rearrange("p (k q) -> p k q", k=4)
                         ).then_inc(S["cat_act"], 1)

            exps(0), exps(1), keep_p(0), keep_p(1), exps(2), keep_heads(0), exps(3), keep_p(2)
            exps(4), keep_p(3), exps(5), keep_p(4), keep_p(5), keep_heads(1)
            scale((10, 11))

            def route(l):
                mod_run((range(10, 12), range(18, 19))[l])
                squares(2 * l + 1)
                if l == 1:
                    mod_run(range(19, 22))
                modulated(2 * l + 1, l, 2, hT)
                for t in range(TT):
                    ins = act.copy(xn_parts[:, 0, t], xn[:, t, :])
                ins.then_inc(S["xn_part1"], 1)
                if l == 0:
                    scale((22, 23))
                act.wait_ge(S["g_shift"], l + 1)
                act.activation(rt_ge, rt_gd, ACT.Exp).then_inc(S["e_group"], 1)
                act.wait_ge(S["e_pair_in"], l + 1)
                act.activation(rt_q, rt_dd, ACT.Exp).then_inc(S["e_pair"], 1)
                for k in range(0, KT, 2):
                    act.wait_ge(S["xg_done"], KT * l + k + 1)
                    act.activation(xgT[:, k, 0:SLOTS], bank[2 + k % 4][:, :], ACT.Identity,
                                   scale=ab[:, l, 2, k:k + 1], bias=ab[:, l, 3, k:k + 1]).then_inc(S["xg_act"], 1)
                if l == 0:
                    mod_run(range(22, 24))

            def experts(l):
                e = E[l]

                def window(j, b):
                    start = act.value_load(win_i[0:1, bass.ds(j, 1)], min_val=0, max_val=SLOTS)
                    if not isinstance(j, int) or j >= 2:
                        act.wait_ge(e["unit_done"], j * UN - UN)
                    act.copy(xw[:, b % 2, :, 0, :], xgT[:, :, bass.ds(start, WIN)]).then_inc(e["xw_part1"], 1)

                def first_parts(j, b, u, loaded):
                    if u == 0:
                        act.wait_ge(gu_in[l][xslot(l, b)], loaded)
                    if not isinstance(j, int) or j * UN + u >= 2:
                        act.wait_ge(e["unit_done"], j * UN + (u - 1))
                    act.copy(parts[:, u % 2, 0].rearrange("p k (w f) -> p w k f", w=2), gu_at(xslot(l, b))[:, :, UT * u:UT * u + UT, :]
                             ).then_inc(e["part1_ready"], 1)

                def keep_part2(j, b):
                    act.wait_ge(e["unit_done"], j * UN + UN)
                    if not isinstance(j, int) or j >= 2:
                        act.wait_ge(e["gu_ready"], j - 1)
                    act.copy(part2[:, b % 2, :], bank[b % 2][WIN:2 * WIN, :]).then_inc(e["part2_kept"], 1)

                def tanh(j, b):
                    act.wait_ge(e["gu_ready"], j + 1)
                    if not isinstance(j, int) or j >= 2:
                        act.wait_ge(e["act_ready"], j - 1)
                    act.activation(th[:, b % 2, :], gu[:, b % 2, 0:FE], ACT.Tanh, scale=0.5).then_inc(e["gu_tanh"], 1)

                def keep_act(j, b):
                    act.wait_ge(e["act_turned"], j + 1)
                    if not isinstance(j, int) or j >= 2:
                        act.wait_ge(e["down_done"], j - 1)
                    act.copy(actT[:, b % 2], bank[2 + b % 2][:, 0:FT * P].rearrange("p (t s) -> p t s", t=FT)[:, :, 0:WIN]).then_inc(e["actT_ready"], 1)

                def keep_y(j, b, signal):
                    start = act.value_load(win_i[0:1, bass.ds(j, 1)], min_val=0, max_val=SLOTS)
                    act.wait_ge(e["down_done"], j + 1)
                    if not isinstance(j, int) or j >= 1:
                        act.wait_ge(e["y_act"], j)
                    act.copy(yT[:, 0:4, bass.ds(start, WIN)], bank[4 + 2 * (b % 2)][:, 0:4 * WIN].rearrange("p (k s) -> p k s", k=4)
                             ).then_inc(signal, 1)

                def group(i):
                    for b in range(XS):
                        j, loaded = i * XS + b, i * 32 + 32
                        n = j if isinstance(i, int) else XS
                        last = i * XS + (b - 1), (b - 1) % XS
                        window(j, b)
                        first_parts(j, b, 0, loaded)
                        if n >= 1:
                            keep_part2(*last)
                        first_parts(j, b, 1, loaded)
                        if n >= 1:
                            tanh(*last)
                        first_parts(j, b, 2, loaded)
                        if n >= 1:
                            keep_act(*last)
                        first_parts(j, b, 3, loaded)
                        if n >= 2:
                            keep_y(i * XS + (b - 2), (b - 2) % XS, e["y_act"])

                act.wait_ge(S["win_ready"], l + 1)
                act.wait_ge(S["xg_act"], 4 * (l + 1))
                act.wait_ge(S["xg_dve"], 4 * (l + 1))
                groups = act.value_load(grp_i[0:1, l:l + 1], min_val=0, max_val=(PASSES - 1) * NE // XS) + NE // XS
                group(0)
                with act.Fori(1, groups) as i:
                    group(i)
                keep_part2(groups * XS - 1, XS - 1)
                keep_y(groups * XS - 2, XS - 2, e["y_act"])
                tanh(groups * XS - 1, XS - 1)
                keep_act(groups * XS - 1, XS - 1)
                keep_y(groups * XS - 1, XS - 1, e["y_last_act"])

            def combine(l):
                for i in range(2):
                    act.wait_ge(S["comb_turned"], 2 * l + i + 1)
                    act.copy(flat(combT[:, 2 * i:2 * i + 2, :]), bank[6 + i][:, :]).then_inc(S["combT_ready"], 1)
                for s in range(4):
                    act.wait_ge(S["y_turned"], 8 * l + 2 * s + 1)
                    act.copy(ysl[:, s, 0:HALF], bank[2 * (s % 2)][:, :]).then_inc(S["ysl_act"], 1)

            route(0)
            experts(0)
            mod_run(range(12, 14))
            combine(0)
            scale((16, 17))
            squares(2)
            mod_run(range(14, 16))
            modulated(2, 1, 0, hp[:, :, PAD:PAD + T])
            scale((18,))
            mod_run(range(16, 18))
            scale((19,))
            route(1)
            experts(1)
            combine(1)
            squares(4)

        @block.vector
        def _(dve):
            own = 0

            def done(ins):
                nonlocal own
                own += 1
                ins.then_inc(S["dve_own"], 1)
                dve.wait_ge(S["dve_own"], own)

            tt, ts, stt = dve.tensor_tensor, dve.tensor_scalar, dve.scalar_tensor_tensor

            def normed(n, write=True):
                dve.wait_ge(S["square_sum"], n + 1)
                ts(stat[:, 2:4], stat[:, 0:2], 1.0 / D, EPS, ALU.mult, ALU.add).then_inc(S["mean_sq"], 1)
                dve.wait_ge(S["inv_rms"], n + 1)
                if write:
                    for t in range(TT):
                        ins = ts(xn[:, t, :], x_res[:, t, :], stat[:, 4 + t:5 + t], None, ALU.mult)
                    ins.then_inc(S["xn_ready"], 1)

            def scale_shift(n, l, which):
                sh, sc = (l, which // 2 * 3), (l, which // 2 * 3 + 1)
                dve.wait_ge(S["col_kept"], columns.index(sc) + 1)
                a, s = raw_col[:, columns.index(sc), :], raw_col[:, columns.index(sh), :]
                if sh in ROW_BIAS:
                    done(dve.tensor_copy(ab[:, l, which + 1, :], s))
                    done(ts(ab[:, l, which, :], a, 1.0, None, ALU.add))
                else:
                    done(tt(ab[:, l, which + 1, :], s, bias_col[:, l, sh[1], :], ALU.add))
                    done(stt(ab[:, l, which, :], a, 1.0, bias_col[:, l, sc[1], :], ALU.add, ALU.add))
                g = {(0, 0): 0, (0, 2): 1, (1, 2): 2, (1, 0): 3}[l, which]
                tt(ab[:, l, which, :], ab[:, l, which, :], gain_col[:, g, :], ALU.mult).then_inc(S["ab_ready"], 1)
                dve.wait_ge(S["ab_ready"], n + 1)

            def modulated(n, l, which, dst):
                for k in range(4, KT):
                    dve.wait_ge(S["xT_done"], 4 * n + k // 2 + 1)
                    ts(dst[:, k, :], bank[2 + k // 2][:, (k % 2) * T:(k % 2 + 1) * T], ab[:, l, which, k:k + 1],
                       ab[:, l, which + 1, k:k + 1], ALU.mult, ALU.add).then_inc(S["hT_dve"], 1)

            def residual(gate, parts, tmp):
                for n, (t, half, b, ready, value) in enumerate(parts):
                    dve.wait_ge(ready, value)
                    at = slice(half * HALF, (half + 1) * HALF)
                    y = tmp[:, (n % 2) * HALF:(n % 2 + 1) * HALF]
                    done(tt(y, bank[b][:, :], gates[:, gate, at], ALU.mult))
                    ins = tt(x_res[:, t, at], x_res[:, t, at], y, ALU.add)
                    if n < 3:
                        done(ins)
                ins.then_inc(S["x_ready"], 1)
                dve.wait_ge(S["x_ready"], {0: 1, 1: 2, 2: 3, 3: 4}[gate])

            def add_up(ms):
                for m in ms:
                    n = chunk_no["mod", m]
                    dve.wait_ge(chunk_in[n % CH], arrivals(n))
                    w = chunk_at(n)
                    done(ts(w[:, KT - 1, :], w[:, KT - 1, :], cs[:, 2, KT - 1:KT], None, ALU.mult))
                    for k in range(on_pe(m), KT - 1):
                        ins = stt(w[:, KT - 1, :], w[:, k, :], cs[:, 2, k:k + 1], w[:, KT - 1, :], ALU.mult, ALU.add)
                        if k < KT - 2:
                            done(ins)
                    ins.then_inc(S["acc_dve"], 1)

            dve.wait_ge(S["c_tanh"], 1)
            done(stt(cs[:, 1, :], cs[:, 1, :], 1.0, cs[:, 0, :], ALU.add, ALU.mult))
            done(ts(cs[:, 2, :], cs[:, 1, :], 0.5, None, ALU.mult))
            dve.tensor_copy(csb, cs[:, 2, :].unsqueeze(2).to_broadcast([P, KT, P])).then_inc(S["csb_ready"], 1)
            normed(0)
            add_up(range(0, 4))
            dve.wait_ge(S["early_in"], 16 * EARLY)
            scale_shift(0, 0, 0)
            modulated(0, 0, 0, hT)
            add_up(range(4, 6))

            dve.wait_ge(S["kv_sq"], 1)
            ts(stat[:, 8:10], stat[:, 6:8], 1.0 / LAT, EPS, ALU.mult, ALU.add).then_inc(S["kv_ms"], 1)
            for t in range(TT):
                a = t * 200 + LAT
                dve.tensor_copy(kidup[:, t, :].rearrange("p (r d) -> p r d", r=2),
                                bank[2][:, a:a + HD].unsqueeze(1).to_broadcast([P, 2, HD]))
                ts(w8[:, t, :], bank[2][:, a + HD:a + HD + H], H ** -0.5, None, ALU.mult)
            dve.wait_ge(S["kv_inv"], 1)
            for t in range(TT):
                ins = ts(kvn[:, t, :], bank[2][:, t * 200:t * 200 + LAT], stat[:, 10 + t:11 + t], None, ALU.mult)
            ins.then_inc(S["kv_ready"], 1)
            dve.wait_ge(S["kt_turned"], 1)
            dve.tensor_copy(kiT, bank[5][:, 0:T]).then_inc(S["kiT_ready"], 1)
            ts(kvnT, bank[5][:, T:2 * T], kvg[:, 0:1], None, ALU.mult).then_inc(S["kvnT_ready"], 1)

            dve.wait_ge(S["kv_ready"], 1)
            for u in range(6):
                t, per, h0 = (0, 4, 4 * u) if u < 2 else (1, 2, 2 * (u - 2))
                span = P if t == 0 else T
                dve.wait_ge(S["score_relu"], u + 1)
                for i in range(per):
                    h, r = h0 + i, relu[:, u % 2, i * span:(i + 1) * span]
                    s, w = score[:, t, 0:span], w8[:, t, head_at(h):head_at(h) + 1]
                    if h == 0:
                        ins = ts(s, r, w, None, ALU.mult)
                    else:
                        ins = stt(s, r, w, s, ALU.mult, ALU.add)
                    if i < per - 1:
                        done(ins)
                ins.then_inc(S["score_added"], 1)
                dve.wait_ge(S["score_added"], u + 1)
            for t in range(TT):
                done(dve.memset(score[0:CHUNK, t, (t + 1) * P - CHUNK:(t + 1) * P], NEVER))

            def gelu_poly(sq, v, after):
                done(ts(sq, sq, GELU_A, 1.0, ALU.mult, ALU.add))
                tt(sq, sq, v, ALU.mult).then_inc(after, 1)

            flat = lambda v: v.rearrange("p a b -> p (a b)")

            def select(t):
                s = score[:, t, 0:(t + 1) * P]
                for r in range(TOPK // 8):
                    done(dve.max(best[:], s))
                    done(dve.match_replace(s, best[:], s, TAKEN))
                done(ts(keep[:, t, 0:(t + 1) * P], s, TAKEN, FAR, ALU.not_equal, ALU.mult))

            select(0)
            select(1)
            add_up(range(6, 8))
            dve.wait_ge(S["gain_row"], 1)
            dve.tensor_copy(gain_col[:, 3, :], bank[2][:, 0:KT]).then_inc(S["gain_ready"], 1)
            dve.wait_ge(S["wsT_copied"], 1)
            dve.memset(wsT[CHUNK:P, :, 0:CHUNK], 0.0).then_inc(S["wsT_ready"], 1)
            dve.wait_ge(S["consts"], 2)
            done(stt(flat(dist), flat(dist), -1.0, flat(dist), ALU.mult, ALU.max))
            dve.wait_ge(S["v_kept"], 2)
            gelu_poly(flat(gtmp), flat(vtk), S["v_poly"])
            add_up(range(8, 10))
            dve.wait_ge(S["v_tanh"], 1)
            done(stt(flat(vtk), flat(gtmp), 1.0, flat(vtk), ALU.add, ALU.mult))
            for t in range(TT):
                done(dve.bn_stats(rt[:, 660 + 6 * t:666 + 6 * t], vtk[:, t, :]))
                done(dve.bn_aggr(rt[:, 680 + 2 * t:682 + 2 * t], rt[:, 660 + 6 * t:666 + 6 * t]))
                ins = ts(stat[:, 16 + t:17 + t], rt[:, 681 + 2 * t:682 + 2 * t], 0.25, EPS, ALU.mult, ALU.add)
            ins.then_inc(S["ln_ms"], 1)
            dve.wait_ge(S["ln_inv"], 1)
            done(ts(stat[:, 18:20], stat[:, 18:20], 0.5, None, ALU.mult))
            for t in range(TT):
                ins = ts(vtk[:, t, :], vtk[:, t, :], rt[:, 680 + 2 * t:681 + 2 * t], stat[:, 18 + t:19 + t],
                         ALU.subtract, ALU.mult)
            ins.then_inc(S["vln_ready"], 1)
            dve.wait_ge(S["u_kept"], 2)
            gelu_poly(flat(usq), flat(uT), S["u_poly"])

            def shift(u):
                dve.wait_ge(S["att_done"], u + 1)
                t, heads = (0, range(4 * u, 4 * u + 4)) if u < 2 else (1, range(2 * u - 4, 2 * u - 2))
                span, b = (P, T)[t], bank[(6, 7, 2)[u % 3]]
                views = [(att0 if t == 0 else att1)[:, h, 0:span] for h in heads]
                for i, (h, a) in enumerate(zip(heads, views)):
                    slope = 2.0 ** (-8.0 * (head_at(h) + 1) / H)
                    ins = stt(a, dist[:, t, 0:span], -slope * HD ** 0.5, b[:, i * span:(i + 1) * span], ALU.mult, ALU.add)
                done(ins)
                for h, a in zip(heads, views):
                    ins = dve.tensor_tensor_reduce(a, a, keep[:, t, 0:span], 1.0, NEVER, ALU.add, ALU.max, amax[:, t, h:h + 1])
                done(ins)
                m = amax[:, t, heads[0]:heads[-1] + 1]
                ts(m, m, -HD ** -0.5, None, ALU.mult).then_inc(S["att_shift"], 1)

            def divide(u):
                dve.wait_ge(S["att_exp"], u + 1)
                t, heads = (0, range(4 * u, 4 * u + 4)) if u < 2 else (1, range(2 * u - 4, 2 * u - 2))
                s = asum[:, t, heads[0]:heads[-1] + 1]
                done(dve.reciprocal(s, s))
                for h in heads:
                    a = (att0 if t == 0 else att1)[:, h, 0:(P, T)[t]]
                    ins = ts(a, a, asum[:, t, h:h + 1], None, ALU.mult)
                ins.then_inc(S["att_ready"], 1)

            def keep_heads(t):
                dve.wait_ge(S["pv_done"], 2 * t + 2)
                dve.tensor_copy(catT[HD:P, 0:4, t * P:(t + 1) * P], bank[4][HD:P, :].rearrange("p (k q) -> p k q", k=4)
                                ).then_inc(S["cat_dve"], 1)

            shift(0), shift(1), divide(0)
            dve.wait_ge(S["u_tanh"], 1)
            stt(flat(uT), flat(usq), 1.0, flat(uT), ALU.add, ALU.mult).then_inc(S["u_ready"], 1)
            dve.wait_ge(S["u_ready"], 1)
            dve.wait_ge(S["sgu_done"], 1)
            for g in range(4):
                src = bank[3 + g // 2][:, (g % 2) * T:(g % 2 + 1) * T].rearrange("p (n i) -> p n i", n=2)
                ins = stt(catT[:, 4 + g, :].rearrange("p (n i) -> p n i", n=2), src, sgug[:, g:g + 1],
                          bsb[:, g, :].unsqueeze(1).to_broadcast([P, 2, P]), ALU.mult, ALU.add)
            done(ins)
            stt(catT[:, 4:8, :], catT[:, 4:8, :], 0.5, uT, ALU.mult, ALU.mult).then_inc(S["bT_ready"], 1)
            shift(2), divide(1), shift(3), divide(2), shift(4), keep_heads(0), divide(3), shift(5), divide(4), divide(5)
            keep_heads(1)
            wo = [chunk_no["out", half] + 1 for half in range(2)]
            residual(0, [(0, 0, 3, S["mix_done"], 1), (1, 0, 4, S["chunk_done"], wo[0]),
                         (0, 1, 6, S["mix_done"], 2), (1, 1, 7, S["chunk_done"], wo[1])], hflat)

            def first_max(oh, src, mx, eq, n):
                done(dve.tensor_reduce(mx, src, AX, ALU.max))
                wide = mx.unsqueeze(2).to_broadcast([P, TT, n])
                done(tt(eq, src, wide, ALU.is_equal))
                done(tt(eq, eq, rank[:, 8 - n:8].unsqueeze(1).to_broadcast([P, TT, n]), ALU.mult))
                done(dve.tensor_reduce(rt_m, eq, AX, ALU.max))
                done(tt(oh, eq, rt_m.unsqueeze(2).to_broadcast([P, TT, n]), ALU.is_equal))

            def route(l):
                if l == 1:
                    add_up((20,))
                normed(2 * l + 1)
                if l == 1:
                    add_up((21,))
                scale_shift(2 * l + 1, l, 2)
                modulated(2 * l + 1, l, 2, hT)
                dve.wait_ge(S["lg_done"], l + 1)
                dve.wait_ge(S["late_in"], 16 * LATE)
                lg = v3(0, RCOLS)
                for t in range(TT):
                    ins = tt(lg[:, t, :], bank[6][:, t * 64:t * 64 + RCOLS], broute[:, l, :], ALU.add)
                done(ins)
                ohg, gmax, pg = v3(94, NG), rt[:, 72:74], rt[:, 92:94]
                first_max(ohg, lg[:, :, 0:NG], gmax, v3(102, NG), NG)
                tt(v3(74, NG), lg[:, :, 0:NG], gmax.unsqueeze(2).to_broadcast([P, TT, NG]), ALU.subtract).then_inc(S["g_shift"], 1)
                el = rt[:, 112:176].rearrange("p (t g e) -> p t g e", t=TT, g=NG)
                for t in range(TT):
                    ins = tt(el[:, t], lg[:, t, NG:RCOLS].rearrange("p (g e) -> p g e", g=NG),
                             ohg[:, t, :].unsqueeze(2).to_broadcast([P, NG, EG]), ALU.mult)
                done(ins)
                eg = v3(176, EG)
                done(dve.tensor_reduce(eg, el.rearrange("p t g e -> p t e g"), AX, ALU.add))
                oh1, oh2, e2, m1, m2 = v3(194, EG), v3(244, EG), v3(226, EG), rt[:, 192:194], rt[:, 242:244]
                first_max(oh1, eg, m1, v3(210, EG), EG)
                done(stt(e2, oh1, FAR, eg, ALU.mult, ALU.add))
                first_max(oh2, e2, m2, v3(210, EG), EG)
                tt(rt_dd, m2, m1, ALU.subtract).then_inc(S["e_pair_in"], 1)
                for oh, a in ((oh1, asg1), (oh2, asg2)):
                    for t in range(TT):
                        ins = tt(a[:, t].rearrange("p (g e) -> p g e", g=NG), ohg[:, t, :].unsqueeze(2).to_broadcast([P, NG, EG]),
                                 oh[:, t, :].unsqueeze(1).to_broadcast([P, NG, EG]), ALU.mult)
                done(ins)
                tt(asg[:], asg1, asg2, ALU.add).then_inc(S["asg_ready"], 1)
                dve.wait_ge(S["e_group"], l + 1)
                done(dve.tensor_reduce(rt[:, 90:92], v3(82, NG), AX, ALU.add))
                done(dve.reciprocal(pg, rt[:, 90:92]))
                dve.wait_ge(S["e_pair"], l + 1)
                g1, g2 = gate1, gate2
                done(ts(rt[:, 264:266], rt_q, 1.0, None, ALU.add))
                done(dve.reciprocal(rt[:, 264:266], rt[:, 264:266]))
                done(tt(g1, pg, rt[:, 264:266], ALU.mult))
                done(tt(g2, g1, rt_q, ALU.mult))
                dve.wait_ge(S["tot_done"], l + 1)
                dve.tensor_copy(tot[0:NE, :], bank[7][0:NE, 64:64 + P]).then_inc(S["tot_ready"], 1)
                dve.wait_ge(S["off_done"], l + 1)
                off, cnt = rt[:, 690:722], rt[:, 722:723]
                done(dve.tensor_copy(off, bank[7][:, 192:192 + NE]))
                done(dve.tensor_reduce(cnt, bank[7][:, 224:224 + NE], AX, ALU.max))
                pos = rt[:, 462:526].rearrange("p (t e) -> p t e", t=TT)
                done(tt(pos, bank[7][:, 0:2 * NE].rearrange("p (t e) -> p t e", t=TT),
                        off.unsqueeze(1).to_broadcast([P, TT, NE]), ALU.add))
                slot = [slot1, slot2]
                for n, a in enumerate((asg1, asg2)):
                    done(tt(a, a, pos, ALU.mult))
                    done(dve.tensor_reduce(slot[n], a, AX, ALU.add))
                for t in range(TT):
                    s1, s2 = slot[0][:, t:t + 1], slot[1][:, t:t + 1]
                    done(ts(pick[:, t, :], slot_no[:], s2, None, ALU.is_equal))
                    ins = stt(sel[:, t, :], slot_no[:], s1, pick[:, t, :], ALU.is_equal, ALU.add)
                ins.then_inc(S["sel_ready"], 1)
                shifts, over = rt[:, 660:660 + PASSES], rt[:, 664:664 + PASSES - 1]
                for p in range(1, PASSES):
                    ins = ts(over[:, p - 1:p], cnt, float(WIN * p), float(WIN), ALU.is_gt, ALU.mult)
                done(ins)
                done(dve.tensor_reduce(shifts[:, 0:1], over, AX, ALU.add))
                for p in range(1, PASSES):
                    ins = ts(shifts[:, p:p + 1], shifts[:, 0:1], -float(WIN * p), None, ALU.add)
                done(ins)
                for p in range(PASSES):
                    ts(win_i[0:1, p * NE:(p + 1) * NE], off[0:1, :], shifts[0:1, p:p + 1], float(SLOTS), ALU.add, ALU.min)
                ts(grp_i[0:1, l:l + 1], shifts[0:1, 0:1], NE / XS / WIN, None, ALU.mult).then_inc(S["win_ready"], 1)
                dve.memset(xgT[:, :, SLOTS:PADDED], 0.0)
                for k in range(1, KT, 2):
                    dve.wait_ge(S["xg_done"], KT * l + k + 1)
                    ts(xgT[:, k, 0:SLOTS], bank[2 + k % 4][:, :], ab[:, l, 2, k:k + 1], ab[:, l, 3, k:k + 1],
                       ALU.mult, ALU.add).then_inc(S["xg_dve"], 1)

            def experts(l):
                e = E[l]

                def window(j, b):
                    start = dve.value_load(win_i[0:1, bass.ds(j, 1)], min_val=0, max_val=SLOTS)
                    dve.wait_ge(e["xw_part1"], j + 1)
                    tt(xw[:, b % 2, :, 1, :], xgT[:, :, bass.ds(start, WIN)], xw[:, b % 2, :, 0, :].bitcast(F32), ALU.subtract
                       ).then_inc(e["xw_ready"], 1)

                def second_parts(j, b, u):
                    dve.wait_ge(e["part1_ready"], j * UN + (u + 1))
                    first, second = (parts[:, u % 2, h].rearrange("p k (w f) -> p w k f", w=2) for h in range(2))
                    tt(second, gu_at(xslot(l, b))[:, :, UT * u:UT * u + UT, :], first.bitcast(F32), ALU.subtract
                       ).then_inc(e["parts_ready"], 1)

                def add_parts(j, b):
                    dve.wait_ge(e["part2_kept"], j + 1)
                    if not isinstance(j, int) or j >= 2:
                        dve.wait_ge(e["act_ready"], j - 1)
                    tt(gu[:, b % 2, :], bank[b % 2][0:WIN, :], part2[:, b % 2, :], ALU.add).then_inc(e["gu_ready"], 1)

                def silu_mul(j, b):
                    dve.wait_ge(e["gu_tanh"], j + 1)
                    dve.wait_ge(e["gu_ready"], j + 1)
                    g, u = gu[:, b % 2, 0:FE], gu[:, b % 2, FE:2 * FE]
                    stt(gl[:, b % 2, :], th[:, b % 2, :], 1.0, g, ALU.add, ALU.mult).then_inc(e["gl_ready"], 1)
                    dve.wait_ge(e["gl_ready"], j + 1)
                    if not isinstance(j, int) or j >= 2:
                        dve.wait_ge(e["act_turned"], j - 1)
                    stt(act_s[0:WIN, b % 2].rearrange("s t p -> s p t"), gl[:, b % 2, :].rearrange("s (p t) -> s p t", t=FT), 0.5,
                        u.rearrange("s (p t) -> s p t", t=FT), ALU.mult, ALU.mult).then_inc(e["act_ready"], 1)

                def keep_y(j, b, signal):
                    start = dve.value_load(win_i[0:1, bass.ds(j, 1)], min_val=0, max_val=SLOTS)
                    dve.wait_ge(e["down_done"], j + 1)
                    if not isinstance(j, int) or j >= 1:
                        dve.wait_ge(e["y_dve"], j)
                    dve.tensor_copy(yT[:, 4:8, bass.ds(start, WIN)], bank[5 + 2 * (b % 2)][:, 0:4 * WIN].rearrange("p (k s) -> p k s", k=4)
                                    ).then_inc(signal, 1)

                def group(i):
                    for b in range(XS):
                        j = i * XS + b
                        n = j if isinstance(i, int) else XS
                        last = i * XS + (b - 1), (b - 1) % XS
                        window(j, b)
                        second_parts(j, b, 0)
                        if n >= 1:
                            add_parts(*last)
                        second_parts(j, b, 1)
                        if n >= 1:
                            silu_mul(*last)
                        second_parts(j, b, 2)
                        second_parts(j, b, 3)
                        if n >= 2:
                            keep_y(i * XS + (b - 2), (b - 2) % XS, e["y_dve"])

                dve.wait_ge(S["win_ready"], l + 1)
                dve.wait_ge(S["xg_act"], 4 * (l + 1))
                dve.wait_ge(S["xg_dve"], 4 * (l + 1))
                dve.wait_ge(S["lg_done"], l + 1)
                groups = dve.value_load(grp_i[0:1, l:l + 1], min_val=0, max_val=(PASSES - 1) * NE // XS) + NE // XS
                group(0)
                with dve.Fori(1, groups) as i:
                    group(i)
                add_parts(groups * XS - 1, XS - 1)
                silu_mul(groups * XS - 1, XS - 1)
                keep_y(groups * XS - 2, XS - 2, e["y_dve"])
                keep_y(groups * XS - 1, XS - 1, e["y_last_dve"])

            def combine(l):
                for s in range(4):
                    dve.wait_ge(S["y_turned"], 8 * l + 2 * s + 2)
                    dve.tensor_copy(ysl[:, s, HALF:D], bank[2 * (s % 2) + 1][:, :]).then_inc(S["ysl_dve"], 1)
                if l == 0:
                    add_up(range(14, 16))
                n = (2, 10)[l]
                residual((1, 3)[l], [(i % 2, i // 2, 4 + i, S["mix_done"], n + i + 1) for i in range(4)], hflat)

            route(0)
            experts(0)
            add_up(range(12, 14))
            combine(0)

            normed(2)
            scale_shift(2, 1, 0)
            done(dve.reciprocal(edge[:], edge[:]))
            dve.memset(hp[:, :, 0:PAD], 0.0)
            dve.memset(sA[:, :, 0:PAD], 0.0)
            done(dve.memset(sB[:, :, 0:PAD], 0.0))
            modulated(2, 1, 0, hp[:, :, PAD:PAD + T])
            dve.wait_ge(S["hT_act"], 12)
            dve.wait_ge(S["hT_dve"], 12)
            src, dst = hp, sA
            for g in range(4):
                step, win = 2 ** g, 2 ** (g + 1)
                done(tt(dst[:, 2 * g:KT, PAD:PAD + T], src[:, 2 * g:KT, PAD:PAD + T],
                        src[:, 2 * g:KT, PAD - step:PAD + T - step], ALU.add))
                y, h = dst[:, 2 * g:2 * g + 2, PAD:PAD + T], hp[:, 2 * g:2 * g + 2, PAD:PAD + T]
                done(stt(hT[:, 2 * g:2 * g + 2, win - 1:T], y[:, :, win - 1:T], 1.0 / win, h[:, :, win - 1:T], ALU.mult, ALU.subtract))
                for i in range(2):
                    done(tt(y[:, i, 0:win - 1], y[:, i, 0:win - 1], edge[:, 0:win - 1], ALU.mult))
                tt(hT[:, 2 * g:2 * g + 2, 0:win - 1], y[:, :, 0:win - 1], h[:, :, 0:win - 1], ALU.subtract
                   ).then_inc(S["pool_ready"], 1)
                src, dst = dst, (sB if g % 2 == 0 else sA)
            dve.wait_ge(S["mod_kept"], turn_of[17] + 1)
            dve.wait_ge(S["row_done"], 1)
            for half in range(2):
                at = slice(half * HALF, (half + 1) * HALF)
                ins = tt(gates[:, 2, at], gates[:, 2, at], bank[2 + half][:, :], ALU.mult)
            done(ins)
            residual(2, [(i % 2, i // 2, 4 + i, S["mix_done"], 6 + i + 1) for i in range(4)], ar(8192, 1024))

            route(1)
            experts(1)
            combine(1)
            normed(4, write=False)
            dve.wait_ge(S["row_done"], 2)
            for t in range(TT):
                for half in range(2):
                    at = slice(half * HALF, (half + 1) * HALF)
                    ins = stt(xn[:, t, at], x_res[:, t, at], stat[:, 4 + t:5 + t], bank[2 + half][:, :], ALU.mult, ALU.mult)
                ins.then_inc(S["out_ready"], 1)


INPUTS = ["x", "c", "w_mod", "b_mod", "norm_mix", "norm_ffn", "w_in", "kv_norm", "w_kv_up", "sgu_norm", "w_s", "b_s", "w_o",
          "w_pool", "pool_scale", "w_gr", "b_gr", "w_er", "b_er", "w_gate", "w_up", "w_down", "norm_out"]


def kernel(**inputs):
    import numpy as np
    import concourse.bacc as bacc
    from concourse.bass_utils import run_bass_kernel_spmd

    nc = bacc.Bacc("TRN2", target_bir_lowering=False, num_devices=1)
    arrays, args = {}, []
    for name in INPUTS:
        a = np.ascontiguousarray(inputs[name])
        arrays[f"in_{name}"] = a
        args.append(nc.dram_tensor(f"in_{name}", a.shape, mybir.dt.from_np(a.dtype), kind="ExternalInput").ap())
    out = nc.dram_tensor("out_0", inputs["x"].shape, F32, kind="ExternalOutput").ap()
    trunk(nc, *args, out)
    r = run_bass_kernel_spmd(nc, [arrays], core_ids=[0])
    return r.results[0]["out_0"]
```
